# Optimizing a Trainium2 kernel written in Bass

```python
import math
import jax, jax.numpy as jnp
from jax import lax
import numpy as np

D_MODEL = 1024
BATCH = 1
SEQ = 256
DEPTH = 1
DEC_BATCH = 8
DEC_SEQ = 1
PAST_LEN = 2048
PAGE_SIZE = 128

D_CONV = D_MODEL
CONV_W = 3
D_SSM = D_MODEL
SSM_H = 16
SSM_GROUPS = D_SSM // SSM_H
STATE_N = 64
DT_MIN = 0.001
DT_MAX = 0.1
N_EXPERTS = 64
TOP_K = 8
N_ROUTE_GROUPS = 8
TOPK_GROUPS = 4
D_EXPERT = 256
D_SHARED = 256
ROUTED_SCALE = 2.5
LN_EPS = 1e-5
ALPHA = (2.0 * DEPTH) ** 0.25
BETA = (8.0 * DEPTH) ** -0.25
D_IN = 3 * D_CONV + D_SSM + 2 * D_MODEL

kernel_name = "hybrid_shortconv_s5_moe_decode_step"

F32 = jnp.float32

def layer_norm(x, g, b):
    xf = x.astype(F32)
    mu = jnp.mean(xf, axis=-1, keepdims=True)
    var = jnp.mean(jnp.square(xf - mu), axis=-1, keepdims=True)
    y = (xf - mu) * lax.rsqrt(var + LN_EPS) * g.astype(F32) + b.astype(F32)
    return y.astype(x.dtype)

def short_conv(u, prev, w):
    L = u.shape[1]
    full = jnp.concatenate([prev.astype(u.dtype), u], axis=1)
    y = full[:, 0:L] * w[0]
    for k in range(1, CONV_W):
        y = y + full[:, k:k + L] * w[k]
    return y, full[:, L:]

def ssm_discretize(a_re, a_im, log_dt):
    dt = jnp.exp(log_dt.astype(F32))[:, None]
    ar = a_re.astype(F32)
    ai = a_im.astype(F32)
    mag = jnp.exp(ar * dt)
    lr = mag * jnp.cos(ai * dt)
    li = mag * jnp.sin(ai * dt)
    den = ar * ar + ai * ai
    fr = ((lr - 1.0) * ar + li * ai) / den
    fi = (li * ar - (lr - 1.0) * ai) / den
    return lr, li, fr, fi

def ssm_combine(e1, e2):
    a1r, a1i, b1r, b1i = e1
    a2r, a2i, b2r, b2i = e2
    return (a2r * a1r - a2i * a1i,
            a2r * a1i + a2i * a1r,
            a2r * b1r - a2i * b1i + b2r,
            a2r * b1i + a2i * b1r + b2i)

def ssm_branch(u, h0r, h0i, a_re, a_im, log_dt, b_re, b_im, c_re, c_im, d_skip):
    bsz, L, _ = u.shape
    uf = u.astype(F32)
    ug = uf.reshape(bsz, L, SSM_GROUPS, SSM_H)
    lr, li, fr, fi = ssm_discretize(a_re, a_im, log_dt)
    br = b_re.astype(F32)
    bi = b_im.astype(F32)
    bbr = fr[..., None] * br - fi[..., None] * bi
    bbi = fr[..., None] * bi + fi[..., None] * br
    xr = jnp.einsum('blgh,gnh->blgn', ug, bbr)
    xi = jnp.einsum('blgh,gnh->blgn', ug, bbi)
    h0r = h0r.astype(F32)
    h0i = h0i.astype(F32)
    xr = xr.at[:, 0].add(lr * h0r - li * h0i)
    xi = xi.at[:, 0].add(lr * h0i + li * h0r)
    ar = jnp.broadcast_to(lr, (1, L) + lr.shape)
    ai = jnp.broadcast_to(li, (1, L) + li.shape)
    _, _, hr, hi = lax.associative_scan(ssm_combine, (ar, ai, xr, xi), axis=1)
    y = (jnp.einsum('blgn,ghn->blgh', hr, c_re.astype(F32))
         - jnp.einsum('blgn,ghn->blgh', hi, c_im.astype(F32)))
    y = y.reshape(bsz, L, D_SSM) + d_skip.astype(F32) * uf
    return y, hr[:, -1], hi[:, -1]

def moe_ffn(x, w_router, router_bias, w_gate, w_up, w_down, ws_gate, ws_up, ws_down):
    bsz, L, D = x.shape
    t = x.reshape(-1, D)
    scores = jax.nn.sigmoid(t.astype(F32) @ w_router.astype(F32))
    biased = scores + router_bias.astype(F32)
    grp = biased.reshape(-1, N_ROUTE_GROUPS, N_EXPERTS // N_ROUTE_GROUPS)
    grp_score = jnp.sum(lax.top_k(grp, 2)[0], axis=-1)
    _, gidx = lax.top_k(grp_score, TOPK_GROUPS)
    gmask = jnp.sum(jax.nn.one_hot(gidx, N_ROUTE_GROUPS, dtype=F32), axis=-2)
    emask = jnp.repeat(gmask, N_EXPERTS // N_ROUTE_GROUPS, axis=-1)
    _, eidx = lax.top_k(jnp.where(emask > 0, biased, -jnp.inf), TOP_K)
    w = jnp.take_along_axis(scores, eidx, axis=-1)
    w = w / jnp.sum(w, axis=-1, keepdims=True) * ROUTED_SCALE
    comb = jnp.sum(jax.nn.one_hot(eidx, N_EXPERTS, dtype=F32) * w[..., None], axis=-2)
    h = jax.nn.silu(jnp.einsum('td,edf->tef', t, w_gate)) * jnp.einsum('td,edf->tef', t, w_up)
    routed = jnp.einsum('tef,efd->td', h * comb[..., None].astype(h.dtype), w_down)
    shared = (jax.nn.silu(t @ ws_gate) * (t @ ws_up)) @ ws_down
    return (routed + shared).reshape(bsz, L, D)

def hybrid_layer(x, conv_prev, h0r, h0i, p):
    split_at = [D_CONV, 2 * D_CONV, 3 * D_CONV, 3 * D_CONV + D_SSM, 3 * D_CONV + D_SSM + D_MODEL]
    proj = x @ p['w_in'] + p['b_in']
    bg, cg, xc, us, ga, gb = jnp.split(proj, split_at, axis=-1)
    conv_out, conv_new = short_conv(cg * xc, conv_prev, p['conv_w'])
    ya = (bg * conv_out) @ p['w_conv_out']
    ys, hr, hi = ssm_branch(us, h0r, h0i, p['a_re'], p['a_im'], p['log_dt'],
                            p['ssm_b_re'], p['ssm_b_im'], p['ssm_c_re'], p['ssm_c_im'], p['ssm_d'])
    z = jax.nn.gelu(ys).astype(x.dtype)
    glu = z * jax.nn.sigmoid(z @ p['w_glu'] + p['b_glu'])
    yb = glu @ p['w_ssm_out']
    m = jax.nn.sigmoid(ga) * ya + jax.nn.sigmoid(gb) * yb
    x = layer_norm(ALPHA * x + m @ p['w_o'], p['ln1_g'], p['ln1_b'])
    f = moe_ffn(x, p['w_router'], p['router_bias'], p['w_gate'], p['w_up'], p['w_down'],
                p['ws_gate'], p['ws_up'], p['ws_down'])
    x = layer_norm(ALPHA * x + f, p['ln2_g'], p['ln2_b'])
    return x, conv_new, hr, hi

def run_trunk(x, conv_st, re_st, im_st, params):
    convs, res, ims = [], [], []
    for l in range(DEPTH):
        p = {k: v[l] for k, v in params.items()}
        x, c, r, i = hybrid_layer(x, conv_st[l], re_st[l], im_st[l], p)
        convs.append(c)
        res.append(r)
        ims.append(i)
    return x, jnp.stack(convs), jnp.stack(res), jnp.stack(ims)

def setup_inputs(seed: int = 0) -> dict:
    key = jax.random.key(seed)
    ks = jax.random.split(key, 33)
    nrm = lambda k, s, sc: jax.random.normal(k, s, F32) * sc
    L_ = DEPTH
    n_idx = jnp.arange(STATE_N, dtype=F32)
    return {
        'x_prompt': nrm(ks[0], (BATCH, SEQ, D_MODEL), 1.0),
        'x_sample': nrm(ks[1], (DEC_BATCH, DEC_SEQ, D_MODEL), 1.0),
        'state_conv': nrm(ks[2], (L_, DEC_BATCH, CONV_W - 1, D_CONV), 0.5),
        'state_ssm_re': nrm(ks[3], (L_, DEC_BATCH, SSM_GROUPS, STATE_N), 0.5),
        'state_ssm_im': nrm(ks[4], (L_, DEC_BATCH, SSM_GROUPS, STATE_N), 0.5),
        'w_in': nrm(ks[5], (L_, D_MODEL, D_IN), D_MODEL ** -0.5),
        'b_in': nrm(ks[6], (L_, D_IN), 0.02),
        'conv_w': nrm(ks[7], (L_, CONV_W, D_CONV), CONV_W ** -0.5),
        'w_conv_out': nrm(ks[8], (L_, D_CONV, D_MODEL), D_CONV ** -0.5),
        'a_re': -0.5 * jnp.exp(nrm(ks[9], (L_, SSM_GROUPS, STATE_N), 0.01)),
        'a_im': math.pi * n_idx + nrm(ks[10], (L_, SSM_GROUPS, STATE_N), 0.01),
        'log_dt': jax.random.uniform(ks[11], (L_, SSM_GROUPS), F32, math.log(DT_MIN), math.log(DT_MAX)),
        'ssm_b_re': nrm(ks[12], (L_, SSM_GROUPS, STATE_N, SSM_H), (2.0 * SSM_H) ** -0.5),
        'ssm_b_im': nrm(ks[13], (L_, SSM_GROUPS, STATE_N, SSM_H), (2.0 * SSM_H) ** -0.5),
        'ssm_c_re': nrm(ks[14], (L_, SSM_GROUPS, SSM_H, STATE_N), STATE_N ** -0.5),
        'ssm_c_im': nrm(ks[15], (L_, SSM_GROUPS, SSM_H, STATE_N), STATE_N ** -0.5),
        'ssm_d': nrm(ks[16], (L_, D_SSM), 1.0),
        'w_glu': nrm(ks[17], (L_, D_SSM, D_SSM), D_SSM ** -0.5),
        'b_glu': nrm(ks[18], (L_, D_SSM), 0.02),
        'w_ssm_out': nrm(ks[19], (L_, D_SSM, D_MODEL), D_SSM ** -0.5),
        'w_o': nrm(ks[20], (L_, D_MODEL, D_MODEL), BETA * D_MODEL ** -0.5),
        'ln1_g': 1.0 + nrm(ks[21], (L_, D_MODEL), 0.02),
        'ln1_b': nrm(ks[22], (L_, D_MODEL), 0.02),
        'w_router': nrm(ks[23], (L_, D_MODEL, N_EXPERTS), D_MODEL ** -0.5),
        'router_bias': nrm(ks[24], (L_, N_EXPERTS), 0.01),
        'w_gate': nrm(ks[25], (L_, N_EXPERTS, D_MODEL, D_EXPERT), D_MODEL ** -0.5),
        'w_up': nrm(ks[26], (L_, N_EXPERTS, D_MODEL, D_EXPERT), D_MODEL ** -0.5),
        'w_down': nrm(ks[27], (L_, N_EXPERTS, D_EXPERT, D_MODEL), BETA * D_EXPERT ** -0.5),
        'ws_gate': nrm(ks[28], (L_, D_MODEL, D_SHARED), D_MODEL ** -0.5),
        'ws_up': nrm(ks[29], (L_, D_MODEL, D_SHARED), D_MODEL ** -0.5),
        'ws_down': nrm(ks[30], (L_, D_SHARED, D_MODEL), BETA * D_SHARED ** -0.5),
        'ln2_g': 1.0 + nrm(ks[31], (L_, D_MODEL), 0.02),
        'ln2_b': nrm(ks[32], (L_, D_MODEL), 0.02),
    }

def reference(x_prompt, x_sample, state_conv, state_ssm_re, state_ssm_im,
              w_in, b_in, conv_w, w_conv_out, a_re, a_im, log_dt,
              ssm_b_re, ssm_b_im, ssm_c_re, ssm_c_im, ssm_d, w_glu, b_glu, w_ssm_out, w_o,
              ln1_g, ln1_b, w_router, router_bias, w_gate, w_up, w_down,
              ws_gate, ws_up, ws_down, ln2_g, ln2_b):
    params = {
        'w_in': w_in, 'b_in': b_in, 'conv_w': conv_w, 'w_conv_out': w_conv_out,
        'a_re': a_re, 'a_im': a_im, 'log_dt': log_dt,
        'ssm_b_re': ssm_b_re, 'ssm_b_im': ssm_b_im, 'ssm_c_re': ssm_c_re, 'ssm_c_im': ssm_c_im,
        'ssm_d': ssm_d, 'w_glu': w_glu, 'b_glu': b_glu, 'w_ssm_out': w_ssm_out, 'w_o': w_o,
        'ln1_g': ln1_g, 'ln1_b': ln1_b, 'w_router': w_router, 'router_bias': router_bias,
        'w_gate': w_gate, 'w_up': w_up, 'w_down': w_down,
        'ws_gate': ws_gate, 'ws_up': ws_up, 'ws_down': ws_down,
        'ln2_g': ln2_g, 'ln2_b': ln2_b,
    }
    bsz = x_prompt.shape[0]
    zero_conv = jnp.zeros((DEPTH, bsz, CONV_W - 1, D_CONV), x_prompt.dtype)
    zero_ssm = jnp.zeros((DEPTH, bsz, SSM_GROUPS, STATE_N), F32)
    y_prompt, conv_p, re_p, im_p = run_trunk(x_prompt, zero_conv, zero_ssm, zero_ssm, params)
    y_sample, conv_s, re_s, im_s = run_trunk(x_sample, state_conv, state_ssm_re, state_ssm_im, params)
    return (y_prompt, y_sample, conv_p, re_p, im_p, conv_s, re_s, im_s)


_drawn_inputs = setup_inputs


def setup_inputs(seed=0):
    import zlib

    import numpy as np

    out = dict(_drawn_inputs(seed))
    spreads = {}
    factors = {'a_re': 8.0, 'b_glu': 7.341, 'ln2_g': 2.892, 'ln2_b': 2.741}
    for name, (base, spread) in spreads.items():
        noise = np.random.default_rng([zlib.crc32(name.encode()), seed]).standard_normal(out[name].shape)
        drawn = base * np.exp(spread * noise) if base else spread * noise
        out[name] = __import__('jax').numpy.asarray(drawn.astype(out[name].dtype))
    for name, factor in factors.items():
        out[name] = (out[name] * factor).astype(out[name].dtype)
    return out
```

```python
from contextlib import ExitStack

import numpy as np

import concourse.bass as bass
from concourse import mybir

ALU = mybir.AluOpType
ACT = mybir.ActivationFunctionType
AX = mybir.AxisListType
F32 = mybir.dt.float32
I32 = mybir.dt.int32

P = 128
D = 1024
KC = D // P
LP = 256
NS = 8
T = LP + NS
G, H, N = 64, 16, 64
NT = G * N // P
PB = P // 32
SEG = 64
NSEG = LP // SEG
HT = NT // 2
HC = KC // 2
E = 64
F = 256
FC = F // P
TOPK, RG, TOPG = 8, 8, 4
EG = E // RG
ROUTED_SCALE = 2.5
EPS = 1e-5
ALPHA = 2.0 ** 0.25
TC = 3

US, CG, XC, BG, GA, GB = range(6)
LOOP_STRIPS = 5 * KC
PER_SEG = LOOP_STRIPS // NSEG
RING = 8

V_BIN = 0
V_BGLU = V_BIN + 6 * KC
V_CW = V_BGLU + KC
V_D = V_CW + 3 * KC
V_LN = V_D + KC
V_ARE = V_LN + 4 * KC
V_AIM = V_ARE + NT
V_LDT = V_AIM + NT
V_RB = V_LDT + NT
NV = V_RB + E

EXP_C = [1.0 / 5040, 1.0 / 720, 1.0 / 120, 1.0 / 24, 1.0 / 6, 0.5, 1.0, 1.0]
LN2_HI, LN2_LO = 0.693359375, -2.12194440e-4
PI2_A, PI2_B, PI2_C = 6.28125, 1.9350051879882812e-03, 3.0199159819567e-07
MAGIC = 12582912.0
GONE = -1e30


class Steps:

    def __init__(self, eng, sem):
        self.eng, self.sem, self.n = eng, sem, 0

    def did(self, ins):
        ins.then_inc(self.sem, 1)
        self.n += 1
        return self.n

    def settle(self):
        self.eng.wait_ge(self.sem, self.n)


def build(nc, x_t, w_front, vecs, b_sm, c_sm, h0, conv_state, w_router, w_gu, w_dn,
          o_y, o_conv_p, o_conv_s, o_ssm_p, o_ssm_s):
    with ExitStack() as ctx:
        def sb(name, shape, dt=F32):
            return ctx.enter_context(nc.sbuf_tensor(name, shape, dt))

        def sem(name):
            return ctx.enter_context(nc.semaphore(name))

        ring = sb("ring", [P, RING, KC, P])
        vec = sb("vec", [P, NV])
        ident = sb("ident", [P, P])
        ones = sb("ones", [P, P])
        xT = sb("xT", [P, KC, T])
        us = sb("us", [P, KC, T])
        proj = sb("proj", [P, 5 * KC, T])
        ys = sb("ys", [P, KC, T])
        cgb, xcb, bgb, gab, gbb = (proj[:, i * KC:(i + 1) * KC, :] for i in range(5))
        cst = sb("cst", [P, KC, 2, NS])
        sml = sb("sml", [P, 24, NT])

        psum = ctx.enter_context(nc.psum_tensor("banks", [P, 8, 512], F32))

        s_vec, s_x, s_bc, s_h0, s_cst = (sem(n) for n in ("vec_loaded", "x_loaded", "bc_loaded", "h0_loaded", "cst_loaded"))
        slot_loaded = [sem(f"slot{i}_loaded") for i in range(RING)]
        strips_done = sem("strips_done")
        bank_free = [sem(f"bank{i}_free") for i in range(2)]
        us_ready = sem("us_ready")
        ident_ready = sem("ident_ready")
        before_ready = sem("before_ready")
        scores_cleared = sem("scores_cleared")
        row_ready = sem("row_ready")
        up_times = sem("up_times")
        pool_own = sem("pool_own")
        dve_own = sem("dve_own")
        dve_loop = sem("dve_loop")
        act_own = sem("act_own")
        angles_ready = sem("angles_ready")
        sines_ready = sem("sines_ready")
        bb_ready = sem("bb_ready")
        bt_turned = sem("bt_turned")
        bt_ready = sem("bt_ready")
        tables_ready = sem("tables_ready")
        negc_ready = sem("negc_ready")
        seg_copied = sem("seg_copied")
        bx_ready = sem("bx_ready")
        demod_done = sem("demod_done")
        xt_ready = sem("xt_ready")
        scan_done = sem("scan_done")
        rot_done = sem("rot_done")
        h_ready = sem("h_ready")
        cy_ready = sem("cy_ready")
        y_evac = sem("y_evac")
        sx_ready = sem("sx_ready")
        sh_ready = sem("sh_ready")
        sy_ready = sem("sy_ready")
        s_fin_ready = sem("final_states_ready")
        ys_ready = sem("ys_ready")
        z_ready = sem("z_ready")
        sg_ready = sem("sg_ready")
        sg_used = sem("sg_used")
        gates_ready = sem("gates_ready")
        v_ready = sem("v_ready")
        u_ready = sem("u_ready")
        glu_ready = sem("glu_ready")
        m_ready = sem("m_ready")
        stat_in = sem("stat_in")
        stat_out = sem("stat_out")
        var_ready = sem("var_ready")
        std_ready = sem("std_ready")
        x1_ready = sem("x1_ready")
        logits_ready = sem("logits_ready")
        scores_ready = sem("scores_ready")
        comb_ready = sem("comb_ready")
        combt_turned = sem("combt_turned")
        combt_ready = sem("combt_ready")
        router_loaded = sem("router_loaded")
        gu_loaded = sem("gu_loaded")
        dn_loaded = sem("dn_loaded")
        gu_used = sem("gu_used")
        silu_done = sem("silu_done")
        h_done = sem("h_done")
        dn_used = sem("dn_used")
        acc_done = sem("acc_done")
        y_ready = sem("y_ready")
        stored = sem("stored")

        N_STORES = 5

        with ExitStack() as fctx:
            def fsb(name, shape, dt=F32):
                return fctx.enter_context(nc.sbuf_tensor(name, shape, dt))

            cosT = fsb("cosT", [P, NT, SEG])
            sinT = fsb("sinT", [P, NT, SEG])
            decay = fsb("decay", [P, NT, SEG])
            prod = fsb("prod", [P, 4, HT, SEG])
            xt = fsb("xt", [P, 2, HT, SEG])
            gg = fsb("gg", [P, 2, HT, SEG])
            hh = fsb("hh", [P, 2, 2, HT, SEG])
            bT = fsb("bT", [P, 2, KC, P])
            cS = fsb("cS", [P, 2, NT, 32])
            seg_u = fsb("seg_u", [P, KC, SEG])
            h0s = fsb("h0s", [P, 2, NT, NS])
            b_in_sm = hh[:, 0].rearrange("p r t s -> p (r t s)").rearrange("p (r t c) -> p r t c", r=2, c=32)
            bb = hh[:, 1].rearrange("p r t s -> p (r t s)").rearrange("p (r t c) -> p r t c", r=2, c=32)
            hs = hh[:, 0].rearrange("p r t s -> p r (t s)")[:, :, 0:NT * NS].rearrange("p r (t b) -> p r t b", b=NS)

            bx = psum[:, 0:4, :].rearrange("p i (c r t) -> p i c r t", c=HC, r=2)

            def bx_half(r):
                return bx[:, :, :, r, :].rearrange("p i c t -> p c i t")

            def by_ci(ap):
                return ap.rearrange("p (c i) t -> p c i t", i=PB)

            with nc.Block() as block:

                @block.sync
                def _(sp):
                    sp.dma_start(vec[:], vecs).then_inc(s_vec, 16)
                    sp.dma_start(xT[:], x_t).then_inc(s_x, 16)
                    sp.dma_start(ring[:, 0], w_front[0]).then_inc(slot_loaded[0], 16)
                    sp.dma_start(b_in_sm, b_sm).then_inc(s_bc, 16)
                    sp.dma_start(cS[:], c_sm).then_inc(s_bc, 16)
                    for n in range(1, KC):
                        sp.dma_start(ring[:, n], w_front[n]).then_inc(slot_loaded[n], 16)
                    sp.dma_start(h0s[:], h0).then_inc(s_h0, 16)
                    sp.dma_start(cst[:], conv_state).then_inc(s_cst, 16)
                    with sp.Fori(0, NSEG) as g:
                        for j in range(PER_SEG):
                            n = g * PER_SEG + (KC + j)
                            sp.wait_ge(strips_done, n - 4)
                            sp.dma_start(ring[:, j % 5], w_front[bass.ds(n, 1)].rearrange("o p f -> (o p) f")).then_inc(slot_loaded[j % 5], 16)
                    with sp.Fori(0, 8) as g:
                        for j in range(4):
                            n = g * 4 + (6 * KC + j)
                            sp.wait_ge(strips_done, n - 3)
                            sp.dma_start(ring[:, j], w_front[bass.ds(n, 1)].rearrange("o p f -> (o p) f")).then_inc(slot_loaded[j], 16)
                    sp.wait_ge(s_fin_ready, 1)
                    sp.dma_start(o_ssm_p, sml[:, 18:20]).then_inc(stored, 16)
                    sp.wait_ge(sh_ready, 2)
                    sp.dma_start(o_ssm_s, hs).then_inc(stored, 16)
                    sp.wait_ge(u_ready, 1)
                    sp.dma_start(o_conv_p, cgb[:, :, LP - 2:LP]).then_inc(stored, 16)
                    sp.dma_start(o_conv_s[:, :, 0], cst[:, :, 1]).then_inc(stored, 16)
                    sp.dma_start(o_conv_s[:, :, 1], cgb[:, :, LP:T]).then_inc(stored, 16)
                    sp.wait_ge(stored, 16 * N_STORES)

                @block.gpsimd
                def _(pool):
                    st = Steps(pool, pool_own)
                    st.did(pool.memset(ones[:], 1.0))
                    st.settle()
                    pool.affine_select(out=ident[:], in_=ones[:], pattern=[[-1, P]], compare_op=ALU.is_equal,
                                       fill=0.0, base=0, channel_multiplier=1).then_inc(ident_ready, 1)
                    pool.wait_ge(s_bc, 32)
                    pool.tensor_scalar(cS[:, 1], cS[:, 1], -1.0, None, ALU.mult).then_inc(negc_ready, 1)
                    with pool.Fori(0, NSEG) as g:
                        for half in range(2):
                            k = g * 2 + half
                            pool.wait_ge(demod_done, k + 1)
                            pool.wait_ge(scan_done, k)
                            pool.tensor_tensor(xt[:, 0], prod[:, 0], prod[:, 1], ALU.add).then_inc(xt_ready, 1)
                            pool.tensor_tensor(xt[:, 1], prod[:, 2], prod[:, 3], ALU.subtract).then_inc(xt_ready, 1)
                            pool.wait_ge(rot_done, k + 1)
                            pool.wait_ge(cy_ready, k)
                            pool.tensor_tensor(hh[:, half, 0], prod[:, 0], prod[:, 1], ALU.subtract).then_inc(h_ready, 1)
                            pool.tensor_tensor(hh[:, half, 1], prod[:, 2], prod[:, 3], ALU.add).then_inc(h_ready, 1)

                @block.scalar
                def _(act):
                    st = Steps(act, act_own)
                    act.wait_ge(s_vec, 16)
                    for n in range(KC):
                        act.wait_ge(strips_done, n + 1)
                        act.activation(us[:, n], psum[:, 5 + n % 2, 0:T], ACT.Identity,
                                       bias=vec[:, V_BIN + n:V_BIN + n + 1]).then_inc(bank_free[n % 2], 1)
                        if n == 0:
                            act.wait_ge(angles_ready, 1)
                            act.activation(sml[:, 8:10], sml[:, 8:10], ACT.Sin).then_inc(sines_ready, 1)
                    act.wait_ge(bank_free[0], KC // 2)
                    act.wait_ge(bank_free[1], KC // 2)
                    act.wait_ge(bt_turned, 1)
                    for r in range(2):
                        act.activation(bT[:, r].rearrange("p (a c) s -> p a (c s)", a=2), psum[:, 2 * r:2 * r + 2, :], ACT.Copy).then_inc(bt_ready, 1)
                    with act.Fori(0, NSEG) as g:
                        act.wait_ge(bx_ready, g * 2)
                        act.activation(seg_u[:], us[:, :, bass.ds(g * SEG, SEG)], ACT.Copy).then_inc(seg_copied, 1)
                        for half in range(2):
                            for j in range(5 * half, 5 * half + 5):
                                s = g * PER_SEG + j
                                act.wait_ge(strips_done, s + (KC + 1))
                                act.activation(proj[:, bass.ds(s, 1), :].rearrange("p o t -> p (o t)"), psum[:, 5 + j % 2, 0:T], ACT.Identity,
                                               bias=vec[:, bass.ds(s + (V_BIN + KC), 1)]).then_inc(bank_free[j % 2], 1)
                            act.wait_ge(cy_ready, g * 2 + (half + 1))
                            act.activation(ys[:, HC * half:HC * half + HC, bass.ds(g * SEG, SEG)],
                                           psum[:, 4, 0:HC * SEG].rearrange("p (c t) -> p c t", c=HC), ACT.Copy).then_inc(y_evac, 1)
                    act.wait_ge(sy_ready, 1)
                    act.activation(ys[:, :, LP:T], psum[:, 4, 0:KC * NS].rearrange("p (c t) -> p c t", c=KC), ACT.Copy).then_inc(y_evac, 1)
                    act.wait_ge(ys_ready, 1)
                    act.activation(ys[:], ys[:], ACT.Gelu_apprx_tanh).then_inc(z_ready, 1)
                    act.wait_ge(bank_free[0], 4 + 5 * NSEG)
                    act.wait_ge(bank_free[1], 4 + 5 * NSEG)
                    act.activation(proj[:, 3 * KC:5 * KC], proj[:, 3 * KC:5 * KC], ACT.Sigmoid).then_inc(gates_ready, 1)
                    for n in range(KC):
                        act.wait_ge(strips_done, 6 * KC + n + 1)
                        act.activation(us[:, n], psum[:, 5 + n % 2, 0:T], ACT.Sigmoid,
                                       bias=vec[:, V_BGLU + n:V_BGLU + n + 1]).then_inc(bank_free[n % 2], 1)

                @block.vector
                def _(dve):
                    st = Steps(dve, dve_own)

                    def do(ins):
                        st.did(ins)
                        st.settle()

                    V = vec
                    a_re, a_im, ldt = (V[:, c:c + NT] for c in (V_ARE, V_AIM, V_LDT))
                    S = [sml[:, i] for i in range(24)]
                    dt_, ard, aid, mag, lr, li, fr, fi = S[0:8]
                    sin_, cos_, t0, t1, t2, t3 = S[8:14]

                    def exp(out, x):
                        do(dve.tensor_scalar(t0, x, 1.4426950408889634, MAGIC, ALU.mult, ALU.add))
                        do(dve.tensor_scalar(t0, t0, -MAGIC, None, ALU.add))
                        do(dve.tensor_scalar(t0, t0, -126.0, 127.0, ALU.max, ALU.min))
                        do(dve.scalar_tensor_tensor(t1, t0, -LN2_HI, x, ALU.mult, ALU.add))
                        do(dve.scalar_tensor_tensor(t1, t0, -LN2_LO, t1, ALU.mult, ALU.add))
                        do(dve.tensor_scalar(t2, t1, EXP_C[0], None, ALU.mult))
                        for c in EXP_C[1:-1]:
                            do(dve.scalar_tensor_tensor(t2, t2, c, t1, ALU.add, ALU.mult))
                        do(dve.tensor_scalar(t3.bitcast(I32), t0, 127.0, 8388608.0, ALU.add, ALU.mult))
                        do(dve.scalar_tensor_tensor(out, t2, EXP_C[-1], t3, ALU.add, ALU.mult))

                    dve.wait_ge(s_vec, 16)
                    exp(dt_, ldt)
                    do(dve.tensor_tensor(ard, a_re, dt_, ALU.mult))
                    do(dve.tensor_tensor(aid, a_im, dt_, ALU.mult))
                    do(dve.tensor_scalar(t0, aid, 0.15915494309189535, MAGIC, ALU.mult, ALU.add))
                    do(dve.tensor_scalar(t0, t0, -MAGIC, None, ALU.add))
                    do(dve.scalar_tensor_tensor(t1, t0, -PI2_A, aid, ALU.mult, ALU.add))
                    do(dve.scalar_tensor_tensor(t1, t0, -PI2_B, t1, ALU.mult, ALU.add))
                    do(dve.scalar_tensor_tensor(t1, t0, -PI2_C, t1, ALU.mult, ALU.add))
                    do(dve.tensor_scalar(sin_, t1, 3.1415925, -3.1415925, ALU.min, ALU.max))
                    do(dve.scalar_tensor_tensor(t2, sin_, -1.0, sin_, ALU.mult, ALU.max))
                    st.did(dve.tensor_scalar(cos_, t2, -1.0, 1.5707963267948966, ALU.mult, ALU.add))
                    st.settle()
                    dve.sem_inc(angles_ready, 1)
                    exp(mag, ard)
                    dve.wait_ge(sines_ready, 1)
                    do(dve.tensor_tensor(lr, mag, cos_, ALU.mult))
                    do(dve.tensor_tensor(li, mag, sin_, ALU.mult))
                    do(dve.tensor_tensor(t0, a_re, a_re, ALU.mult))
                    do(dve.tensor_tensor(t1, a_im, a_im, ALU.mult))
                    do(dve.tensor_tensor(t0, t0, t1, ALU.add))
                    do(dve.reciprocal(t0, t0))
                    do(dve.tensor_scalar(t1, lr, -1.0, None, ALU.add))
                    do(dve.tensor_tensor(t2, t1, a_re, ALU.mult))
                    do(dve.tensor_tensor(t3, li, a_im, ALU.mult))
                    do(dve.tensor_tensor(t2, t2, t3, ALU.add))
                    do(dve.tensor_tensor(fr, t2, t0, ALU.mult))
                    do(dve.tensor_tensor(t2, li, a_re, ALU.mult))
                    do(dve.tensor_tensor(t3, t1, a_im, ALU.mult))
                    do(dve.tensor_tensor(t2, t2, t3, ALU.subtract))
                    do(dve.tensor_tensor(fi, t2, t0, ALU.mult))

                    def wide(v, m):
                        return v.rearrange("p (t o) -> p t o", o=1).broadcast_to([P, NT, m])

                    dve.wait_ge(s_bc, 32)
                    tmp = prod[:, 0].rearrange("p t s -> p (t s)").rearrange("p (t c) -> p t c", c=32)
                    frw, fiw = wide(fr, 32), wide(fi, 32)
                    do(dve.tensor_tensor(tmp, b_in_sm[:, 1], fiw, ALU.mult))
                    do(dve.tensor_tensor(bb[:, 0], b_in_sm[:, 0], frw, ALU.mult))
                    do(dve.tensor_tensor(bb[:, 0], bb[:, 0], tmp, ALU.subtract))
                    do(dve.tensor_tensor(tmp, b_in_sm[:, 0], fiw, ALU.mult))
                    do(dve.tensor_tensor(bb[:, 1], b_in_sm[:, 1], frw, ALU.mult))
                    dve.tensor_tensor(bb[:, 1], bb[:, 1], tmp, ALU.add).then_inc(bb_ready, 1)

                    do(dve.memset(cosT[:, :, 0:1], 1.0))
                    do(dve.memset(sinT[:, :, 0:1], 0.0))
                    vc, vs, wc, ws = cos_, sin_, S[14], S[15]
                    m = 1
                    while m < SEG:
                        c0, s0 = cosT[:, :, 0:m], sinT[:, :, 0:m]
                        c1, s1 = cosT[:, :, m:2 * m], sinT[:, :, m:2 * m]
                        pa = prod[:, 0:2].rearrange("p a t s -> p (a t) s")[:, :, 0:m]
                        pb = prod[:, 2:4].rearrange("p a t s -> p (a t) s")[:, :, 0:m]
                        st.did(dve.tensor_tensor(c1, c0, wide(vc, m), ALU.mult))
                        st.did(dve.tensor_tensor(pa, s0, wide(vs, m), ALU.mult))
                        st.did(dve.tensor_tensor(s1, s0, wide(vc, m), ALU.mult))
                        do(dve.tensor_tensor(pb, c0, wide(vs, m), ALU.mult))
                        st.did(dve.tensor_tensor(c1, c1, pa, ALU.subtract))
                        st.did(dve.tensor_tensor(s1, s1, pb, ALU.add))
                        st.did(dve.tensor_tensor(t0, vc, vc, ALU.mult))
                        st.did(dve.tensor_tensor(t1, vs, vs, ALU.mult))
                        do(dve.tensor_tensor(t2, vc, vs, ALU.mult))
                        st.did(dve.tensor_tensor(wc, t0, t1, ALU.subtract))
                        do(dve.tensor_scalar(ws, t2, 2.0, None, ALU.mult))
                        vc, vs, wc, ws = wc, ws, (S[16] if wc is S[14] else S[14]), (S[17] if ws is S[15] else S[15])
                        m *= 2
                    do(dve.tensor_copy(decay[:], wide(mag, SEG)))
                    dve.memset(decay[:, :, 0:1], 0.0).then_inc(tables_ready, 1)
                    dve.wait_ge(tables_ready, 1)

                    dve.wait_ge(bt_turned, 1)
                    for half in range(2):
                        do(dve.memset(hh[:, half, :, :, SEG - 1:SEG], 0.0))
                    with dve.Fori(0, NSEG) as g:
                        for half in range(2):
                            k = g * 2 + half
                            tiles = slice(HT * half, HT * half + HT)
                            ct, sn = by_ci(cosT[:, tiles]), by_ci(sinT[:, tiles])
                            dve.wait_ge(bx_ready, k + 1)
                            dve.wait_ge(h_ready, k * 2)
                            dve.tensor_tensor(by_ci(prod[:, 0]), bx_half(0), ct, ALU.mult)
                            dve.tensor_tensor(by_ci(prod[:, 1]), bx_half(1), sn, ALU.mult)
                            dve.tensor_tensor(by_ci(prod[:, 2]), bx_half(1), ct, ALU.mult)
                            dve.tensor_tensor(by_ci(prod[:, 3]), bx_half(0), sn, ALU.mult).then_inc(demod_done, 1)
                            base = g * (2 * 6) + 6 * half
                            c = sml[:, 18:22, 0:HT]
                            hr, hi = hh[:, half, 0, :, SEG - 1], hh[:, half, 1, :, SEG - 1]
                            lrh, lih = lr[:, tiles], li[:, tiles]
                            first = [xt[:, 0, :, 0], xt[:, 1, :, 0]]
                            dve.tensor_tensor(c[:, 0], lrh, hr, ALU.mult).then_inc(dve_loop, 1)
                            dve.tensor_tensor(c[:, 1], lih, hi, ALU.mult).then_inc(dve_loop, 1)
                            dve.tensor_tensor(c[:, 2], lrh, hi, ALU.mult).then_inc(dve_loop, 1)
                            dve.tensor_tensor(c[:, 3], lih, hr, ALU.mult).then_inc(dve_loop, 1)
                            dve.wait_ge(dve_loop, base + 4)
                            dve.tensor_tensor(c[:, 0], c[:, 0], c[:, 1], ALU.subtract).then_inc(dve_loop, 1)
                            dve.tensor_tensor(c[:, 2], c[:, 2], c[:, 3], ALU.add).then_inc(dve_loop, 1)
                            dve.wait_ge(dve_loop, base + 6)
                            dve.wait_ge(xt_ready, k * 2 + 2)
                            dve.tensor_tensor(first[0], first[0], c[:, 0], ALU.add).then_inc(sx_ready, 1)
                            dve.tensor_tensor(first[1], first[1], c[:, 2], ALU.add).then_inc(sx_ready, 1)
                            dve.wait_ge(sx_ready, k * 2 + 2)
                            dec = decay[:, tiles].rearrange("p t s -> p (t s)")
                            for r in range(2):
                                ins = dve.tensor_tensor_scan(gg[:, r].rearrange("p t s -> p (t s)"), dec,
                                                             xt[:, r].rearrange("p t s -> p (t s)"), 0.0, ALU.mult, ALU.add)
                            ins.then_inc(scan_done, 1)
                            dve.wait_ge(scan_done, k + 1)
                            ct, sn = cosT[:, tiles], sinT[:, tiles]
                            dve.tensor_tensor(prod[:, 0], gg[:, 0], ct, ALU.mult)
                            dve.tensor_tensor(prod[:, 1], gg[:, 1], sn, ALU.mult)
                            dve.tensor_tensor(prod[:, 2], gg[:, 1], ct, ALU.mult)
                            dve.tensor_tensor(prod[:, 3], gg[:, 0], sn, ALU.mult).then_inc(rot_done, 1)
                    fin = sml[:, 18:20]
                    dve.wait_ge(h_ready, 4 * NSEG)
                    for r in range(2):
                        for half in range(2):
                            do(dve.tensor_copy(fin[:, r, half * HT:half * HT + HT], hh[:, half, r, :, SEG - 1]))
                    dve.sem_inc(s_fin_ready, 1)
                    dve.wait_ge(s_h0, 16)
                    dve.wait_ge(cy_ready, 2 * NSEG)
                    q = [prod[:, i].rearrange("p t s -> p (t s)")[:, 0:NT * NS].rearrange("p (t b) -> p t b", b=NS) for i in range(4)]
                    do(dve.tensor_tensor(q[0], h0s[:, 0], wide(lr, NS), ALU.mult))
                    do(dve.tensor_tensor(q[1], h0s[:, 1], wide(li, NS), ALU.mult))
                    do(dve.tensor_tensor(q[2], h0s[:, 1], wide(lr, NS), ALU.mult))
                    do(dve.tensor_tensor(q[3], h0s[:, 0], wide(li, NS), ALU.mult))
                    do(dve.tensor_tensor(q[0], q[0], q[1], ALU.subtract))
                    do(dve.tensor_tensor(q[2], q[2], q[3], ALU.add))
                    dve.wait_ge(bx_ready, 2 * NSEG + 1)
                    sx = psum[:, 0:4, 0:2 * KC * NS].rearrange("p i (c r b) -> p i c r b", c=KC, r=2)
                    for r in range(2):
                        dve.tensor_tensor(by_ci(hs[:, r]), sx[:, :, :, r, :].rearrange("p i c b -> p c i b"),
                                          by_ci(q[2 * r]), ALU.add).then_inc(sh_ready, 1)
                    dve.wait_ge(y_evac, 2 * NSEG + 1)
                    for n in range(KC):
                        st.did(dve.scalar_tensor_tensor(ys[:, n], us[:, n], V[:, V_D + n:V_D + n + 1], ys[:, n], ALU.mult, ALU.add))
                    st.settle()
                    dve.sem_inc(ys_ready, 1)
                    dve.wait_ge(bank_free[0], 4 + 5 * NSEG)
                    dve.wait_ge(bank_free[1], 4 + 5 * NSEG)
                    dve.wait_ge(s_cst, 16)
                    do(dve.tensor_tensor(cgb, cgb, xcb, ALU.mult))
                    dve.sem_inc(u_ready, 1)

                    def cw(k, n):
                        return V[:, V_CW + k * KC + n:V_CW + k * KC + n + 1]

                    for n in range(KC):
                        st.did(dve.tensor_scalar(xcb[:, n], cgb[:, n], cw(2, n), None, ALU.mult))
                    st.settle()
                    for n in range(KC):
                        st.did(dve.scalar_tensor_tensor(xcb[:, n, 1:LP], cgb[:, n, 0:LP - 1], cw(1, n), xcb[:, n, 1:LP], ALU.mult, ALU.add))
                        st.did(dve.scalar_tensor_tensor(xcb[:, n, LP:T], cst[:, n, 1], cw(1, n), xcb[:, n, LP:T], ALU.mult, ALU.add))
                    st.settle()
                    for n in range(KC):
                        st.did(dve.scalar_tensor_tensor(xcb[:, n, 2:LP], cgb[:, n, 0:LP - 2], cw(0, n), xcb[:, n, 2:LP], ALU.mult, ALU.add))
                        st.did(dve.scalar_tensor_tensor(xcb[:, n, LP:T], cst[:, n, 0], cw(0, n), xcb[:, n, LP:T], ALU.mult, ALU.add))
                    st.settle()
                    do(dve.tensor_tensor(xcb, xcb, bgb, ALU.mult))
                    dve.sem_inc(v_ready, 1)
                    for n in range(KC):
                        dve.wait_ge(bank_free[n % 2], 4 + 5 * NSEG + n // 2 + 1)
                        st.did(dve.tensor_tensor(us[:, n], ys[:, n], us[:, n], ALU.mult))
                    st.settle()
                    dve.sem_inc(glu_ready, 1)
                    dve.wait_ge(gates_ready, 1)
                    for n in range(KC):
                        dve.wait_ge(strips_done, 7 * KC + n + 1)
                        dve.tensor_tensor(bgb[:, n], psum[:, 5 + n % 2, 0:T], gab[:, n], ALU.mult).then_inc(bank_free[n % 2], 1)
                    for n in range(KC):
                        dve.wait_ge(strips_done, 8 * KC + n + 1)
                        dve.tensor_tensor(gbb[:, n], psum[:, 5 + n % 2, 0:T], gbb[:, n], ALU.mult).then_inc(bank_free[n % 2], 1)
                        dve.wait_ge(bank_free[n % 2], 4 + 5 * NSEG + 4 + 4 + n // 2 + 1)
                        do(dve.tensor_tensor(ys[:, n], gbb[:, n], bgb[:, n], ALU.add))
                    dve.sem_inc(m_ready, 1)
                    for n in range(KC):
                        dve.wait_ge(strips_done, 9 * KC + n + 1)
                        dve.scalar_tensor_tensor(xcb[:, n], xT[:, n], ALPHA, psum[:, 5 + n % 2, 0:T], ALU.mult, ALU.add).then_inc(bank_free[n % 2], 1)

                @block.tensor
                def _(pe):
                    def strip(slot, loads, n2, par, rhs):
                        pe.wait_ge(slot_loaded[slot], loads)
                        pe.wait_ge(bank_free[par], n2)
                        for k in range(KC):
                            ins = pe.matmul(psum[:, 5 + par, 0:T], ring[:, slot, k], rhs[:, k], start=(k == 0), stop=(k == KC - 1))
                        ins.then_inc(strips_done, 1)

                    pe.wait_ge(s_x, 16)
                    for n in range(KC):
                        pe.wait_ge(slot_loaded[n], 16)
                        if n >= 2:
                            pe.wait_ge(bank_free[n % 2], n // 2)
                        for k in range(KC):
                            ins = pe.matmul(psum[:, 5 + n % 2, 0:T], ring[:, n, k], xT[:, k], start=(k == 0), stop=(k == KC - 1))
                        ins.then_inc(strips_done, 1)
                    pe.wait_ge(ident_ready, 1)
                    pe.wait_ge(bb_ready, 1)
                    for r in range(2):
                        for c in range(KC):
                            ins = pe.transpose(psum[:, 2 * r + c // 4, (c % 4) * P:(c % 4) * P + P],
                                               bb[:, r, PB * c:PB * c + PB].rearrange("p t c -> p (t c)"), ident[:])
                    ins.then_inc(bt_turned, 1)
                    pe.wait_ge(bt_ready, 2)
                    pe.wait_ge(negc_ready, 1)
                    pe.wait_ge(bank_free[0], KC // 2)
                    pe.wait_ge(bank_free[1], KC // 2)
                    with pe.Fori(0, NSEG) as g:
                        for half in range(2):
                            k = g * 2 + half
                            if half == 0:
                                pe.wait_ge(seg_copied, g + 1)
                            pe.wait_ge(demod_done, k)
                            for c in range(HC):
                                for i in range(PB):
                                    rows = slice(32 * i, 32 * i + 32)
                                    for r in range(2):
                                        ins = pe.matmul(bx[:, i, c, r, :], bT[rows, r, HC * half + c, :], seg_u[rows, HC * half + c, :],
                                                        start=True, stop=True)
                            ins.then_inc(bx_ready, 1)
                            for j in range(5 * half, 5 * half + 5):
                                n2 = g * 5 + (4 + j // 2)
                                strip(j % 5, g * 32 + (32 + 16 * (j // 5)), n2, j % 2, xT)
                            pe.wait_ge(h_ready, k * 2 + 2)
                            pe.wait_ge(y_evac, k)
                            for c in range(HC):
                                for i in range(PB):
                                    t = PB * c + i
                                    for r in range(2):
                                        ins = pe.matmul(psum[32 * i:32 * i + 32, 4, SEG * c:SEG * c + SEG], cS[:, r, HT * half + t],
                                                        hh[:, half, r, t], start=(r == 0), stop=(r == 1))
                            ins.then_inc(cy_ready, 1)
                    pe.wait_ge(demod_done, 2 * NSEG)
                    sx = psum[:, 0:4, 0:2 * KC * NS].rearrange("p i (c r b) -> p i c r b", c=KC, r=2)
                    for c in range(KC):
                        for i in range(PB):
                            rows = slice(32 * i, 32 * i + 32)
                            for r in range(2):
                                ins = pe.matmul(sx[:, i, c, r, :], bT[rows, r, c, :], us[rows, c, LP:T], start=True, stop=True)
                    ins.then_inc(bx_ready, 1)
                    pe.wait_ge(sh_ready, 2)
                    pe.wait_ge(y_evac, 2 * NSEG)
                    for c in range(KC):
                        for i in range(PB):
                            for r in range(2):
                                ins = pe.matmul(psum[32 * i:32 * i + 32, 4, NS * c:NS * c + NS], cS[:, r, PB * c + i], hs[:, r, PB * c + i],
                                                start=(r == 0), stop=(r == 1))
                    ins.then_inc(sy_ready, 1)
                    for layer, (rhs, ready) in enumerate(((ys, z_ready), (xcb, v_ready), (us, glu_ready), (ys, m_ready))):
                        pe.wait_ge(ready, 1)
                        with pe.Fori(0, 2) as g:
                            for j in range(4):
                                strip(j, g * 16 + (16 * (1 + 2 * NSEG + 2 * layer + 1)), g * 2 + (4 + 5 * NSEG + 4 * layer + j // 2), j % 2, rhs)

        r_ = xcb
        gu = sb("gu", [P, KC, 2 * F])
        dn = sb("dn", [P, FC, D])
        wr = sb("wr", [P, KC, E])
        sq = sb("sq", [P, KC, T])
        mu = sb("mu", [P, 3, T])
        scores = sb("scores", [P, TC, E])
        rt = sb("rt", [P, 8, TC, E])
        cmp = sb("cmp", [P, TC, RG, RG])
        before = sb("before", [P, RG, RG])
        top8 = sb("top8", [P, TC, RG, 8])
        combT = sb("combT", [P, T])
        row = sb("row", [P, T])
        hT = sb("hT", [P, FC, T])
        sil = sb("sil", [P, FC, T])
        x1 = cgb
        acc = gab
        y = gbb
        tok = [P, P, NS]

        with nc.Block() as block:

            @block.sync
            def _(sp):
                sp.dma_start(wr[:], w_router).then_inc(router_loaded, 16)
                sp.dma_start(gu[:], w_gu[0]).then_inc(gu_loaded, 16)
                sp.dma_start(dn[:], w_dn[0]).then_inc(dn_loaded, 16)
                with sp.Fori(1, E + 1) as e:
                    sp.wait_ge(gu_used, e)
                    sp.dma_start(gu[:], w_gu[bass.ds(e, 1)].rearrange("o p f -> (o p) f")).then_inc(gu_loaded, 16)
                    sp.wait_ge(dn_used, e * 8)
                    sp.dma_start(dn[:], w_dn[bass.ds(e, 1)].rearrange("o p f -> (o p) f")).then_inc(dn_loaded, 16)
                sp.wait_ge(y_ready, 1)
                sp.dma_start(o_y, y).then_inc(stored, 16)
                sp.wait_ge(stored, 16 * (N_STORES + 1))

            @block.gpsimd
            def _(pool):
                pool.affine_select(out=before[:], in_=ones[:, 0:RG * RG].rearrange("p (g h) -> p g h", g=RG), pattern=[[1, RG], [-1, RG]],
                                   compare_op=ALU.is_gt, fill=0.0, base=0, channel_multiplier=0).then_inc(before_ready, 1)

            @block.scalar
            def _(act):
                def layer_norm(first):
                    act.wait_ge(var_ready, first + 1)
                    act.activation(mu[:, 1], mu[:, 1], ACT.Sqrt).then_inc(std_ready, 1)

                layer_norm(0)
                act.wait_ge(scores_cleared, 1)
                act.wait_ge(logits_ready, TC)
                for c in range(TC):
                    act.activation(scores[0:tok[c], c], psum[0:tok[c], 7, c * E:c * E + E], ACT.Sigmoid).then_inc(scores_ready, 1)
                act.wait_ge(combt_ready, 1)
                with act.Fori(0, E + 1) as e:
                    act.wait_ge(gu_used, e)
                    act.activation(row[:], combT[:], ACT.Copy, scale=ident[:, bass.ds(e, 1)]).then_inc(row_ready, 1)
                    act.wait_ge(gu_used, e + 1)
                    act.wait_ge(h_done, e * 2)
                    for f in range(FC):
                        act.activation(sil[:, f], psum[:, f, 0:T], ACT.Silu).then_inc(silu_done, 1)
                layer_norm(1)

            @block.vector
            def _(dve):
                st = Steps(dve, dve_loop)
                st.n = 12 * NSEG

                def do(ins):
                    st.did(ins)
                    st.settle()

                def layer_norm(src, out, which):
                    wide = mu[:, 0:1].broadcast_to([P, KC, T])
                    dve.wait_ge(stat_out, 2 * which + 1)
                    do(dve.tensor_scalar(mu[:, 0], psum[:, 4, 0:T], 1.0 / D, None, ALU.mult))
                    do(dve.tensor_tensor(src, src, wide, ALU.subtract))
                    do(dve.tensor_tensor(sq[:], src, src, ALU.mult))
                    dve.sem_inc(stat_in, 1)
                    dve.wait_ge(stat_out, 2 * which + 2)
                    do(dve.tensor_scalar(mu[:, 0], psum[:, 4, 0:T], 1.0 / D, EPS, ALU.mult, ALU.add))
                    do(dve.reciprocal(mu[:, 1], mu[:, 0]))
                    dve.sem_inc(var_ready, 1)
                    dve.wait_ge(std_ready, which + 1)
                    do(dve.tensor_tensor(mu[:, 2], mu[:, 1], mu[:, 1], ALU.mult))
                    do(dve.tensor_tensor(mu[:, 2], mu[:, 2], mu[:, 0], ALU.mult))
                    do(dve.tensor_scalar(mu[:, 2], mu[:, 2], -0.5, 1.5, ALU.mult, ALU.add))
                    do(dve.tensor_tensor(mu[:, 0], mu[:, 2], mu[:, 1], ALU.mult))
                    do(dve.tensor_tensor(src, src, wide, ALU.mult))
                    v = V_LN + 2 * KC * which
                    for n in range(KC):
                        st.did(dve.tensor_scalar(out[:, n], src[:, n], vec[:, v + n:v + n + 1], vec[:, v + KC + n:v + KC + n + 1], ALU.mult, ALU.add))
                    st.settle()

                layer_norm(r_, x1, 0)
                dve.sem_inc(x1_ready, 1)
                do(dve.tensor_scalar(acc, x1, ALPHA, None, ALU.mult))
                biased, masked, left, picked, wts, tmp = (rt[:, i] for i in range(6))
                gs, rank, cnt = rt[:, 6, :, 0:RG], rt[:, 6, :, RG:2 * RG], rt[:, 7, :, 0:RG]
                total = rt[:, 7, :, RG:RG + 1]
                dve.memset(scores[:], 0.5).then_inc(scores_cleared, 1)
                dve.wait_ge(scores_ready, TC)
                rb = vec[:, V_RB:V_RB + E].rearrange("p (o e) -> p o e", o=1).broadcast_to([P, TC, E])
                do(dve.tensor_tensor(biased, scores[:], rb, ALU.add))
                for c in range(TC):
                    for g in range(RG):
                        st.did(dve.max(top8[:, c, g], biased[:, c, g * EG:g * EG + EG]))
                st.settle()
                do(dve.tensor_tensor(gs, top8[:, :, :, 0], top8[:, :, :, 1], ALU.add))
                dve.wait_ge(before_ready, 1)
                for c in range(TC):
                    me = gs[:, c].rearrange("p (g o) -> p g o", o=1).broadcast_to([P, RG, RG])
                    other = gs[:, c].rearrange("p (o g) -> p o g", o=1).broadcast_to([P, RG, RG])
                    eq = cmp[:, c]
                    do(dve.tensor_tensor(eq, other, me, ALU.is_equal))
                    do(dve.tensor_tensor(eq, eq, before[:], ALU.mult))
                    do(dve.tensor_reduce(cnt[:, c], eq, AX.X, ALU.add))
                    do(dve.tensor_tensor(eq, other, me, ALU.is_gt))
                    do(dve.tensor_reduce(rank[:, c], eq, AX.X, ALU.add))
                do(dve.tensor_tensor(rank, rank, cnt, ALU.add))
                do(dve.tensor_scalar(rank, rank, float(TOPG), None, ALU.is_lt))
                do(dve.tensor_scalar(rank, rank, -GONE, GONE, ALU.mult, ALU.add))
                for c in range(TC):
                    gm = rank[:, c].rearrange("p (g o) -> p g o", o=1).broadcast_to([P, RG, EG])
                    do(dve.tensor_tensor(masked[:, c].rearrange("p (g e) -> p g e", g=RG), biased[:, c].rearrange("p (g e) -> p g e", g=RG), gm, ALU.add))
                    do(dve.max(top8[:, c, 0], masked[:, c]))
                    do(dve.match_replace(left[:, c], top8[:, c, 0], masked[:, c], 3 * GONE))
                do(dve.tensor_tensor(picked, left, masked, ALU.not_equal))
                do(dve.tensor_tensor(wts, scores[:], picked, ALU.mult))
                do(dve.tensor_reduce(total, wts, AX.X, ALU.add))
                do(dve.reciprocal(total, total))
                for c in range(TC):
                    do(dve.tensor_scalar(wts[:, c], wts[:, c], total[:, c], ROUTED_SCALE, ALU.mult, ALU.mult))
                dve.sem_inc(comb_ready, 1)
                do(dve.memset(combT[:], 1.0))
                dve.wait_ge(combt_turned, 1)
                st.did(dve.tensor_copy(combT[0:E, :], psum[0:E, 7, 0:T]))
                st.settle()
                dve.sem_inc(combt_ready, 1)
                with dve.Fori(0, E + 1) as e:
                    dve.wait_ge(gu_used, e + 1)
                    for f in range(FC):
                        dve.wait_ge(silu_done, e * 2 + (f + 1))
                        dve.tensor_tensor(sil[:, f], sil[:, f], psum[:, FC + f, 0:T], ALU.mult).then_inc(up_times, 1)
                    dve.wait_ge(up_times, e * 2 + 2)
                    dve.wait_ge(dn_used, e * 8)
                    for f in range(FC):
                        dve.tensor_tensor(hT[:, f], sil[:, f], psum[:, 4, 0:T], ALU.mult).then_inc(h_done, 1)
                    for n in range(KC):
                        dve.wait_ge(dn_used, e * 8 + (n + 1))
                        dve.tensor_tensor(acc[:, n], acc[:, n], psum[:, 5 + n % 2, 0:T], ALU.add).then_inc(acc_done, 1)
                dve.wait_ge(acc_done, 8 * (E + 1))
                dve.sem_inc(stat_in, 1)
                layer_norm(acc, y, 1)
                dve.sem_inc(y_ready, 1)

            @block.tensor
            def _(pe):
                def column_sums(src):
                    for k in range(KC):
                        ins = pe.matmul(psum[:, 4, 0:T], ones[:], src[:, k], start=(k == 0), stop=(k == KC - 1))
                    ins.then_inc(stat_out, 1)

                for b in range(2):
                    pe.wait_ge(bank_free[b], 4 + 5 * NSEG + 16)
                column_sums(r_)
                pe.wait_ge(stat_in, 1)
                column_sums(sq)
                pe.wait_ge(x1_ready, 1)
                pe.wait_ge(router_loaded, 16)
                for c in range(TC):
                    for k in range(KC):
                        ins = pe.matmul(psum[0:tok[c], 7, c * E:c * E + E], x1[:, k, c * P:c * P + tok[c]], wr[:, k], start=(k == 0), stop=(k == KC - 1))
                    ins.then_inc(logits_ready, 1)
                pe.wait_ge(comb_ready, 1)
                pe.wait_ge(scores_ready, TC)
                for c in range(TC):
                    ins = pe.transpose(psum[0:E, 7, c * P:c * P + tok[c]], rt[0:tok[c], 4, c], ident[0:tok[c], 0:tok[c]])
                ins.then_inc(combt_turned, 1)
                pe.wait_ge(combt_ready, 1)
                with pe.Fori(0, E + 1) as e:
                    pe.wait_ge(gu_loaded, e * 16 + 16)
                    pe.wait_ge(h_done, e * 2)
                    for f in range(2 * FC):
                        for k in range(KC):
                            pe.matmul(psum[:, f, 0:T], gu[:, k, f * P:f * P + P], x1[:, k], start=(k == 0), stop=(k == KC - 1))
                    pe.wait_ge(row_ready, e + 1)
                    ins = pe.matmul(psum[:, 4, 0:T], ones[:], row[:], start=True, stop=True)
                    ins.then_inc(gu_used, 1)
                    pe.wait_ge(dn_loaded, e * 16 + 16)
                    pe.wait_ge(h_done, e * 2 + 2)
                    for n in range(KC):
                        if n >= 2:
                            pe.wait_ge(acc_done, e * 8 + (n - 1))
                        else:
                            pe.wait_ge(acc_done, e * 8)
                        for f in range(FC):
                            ins = pe.matmul(psum[:, 5 + n % 2, 0:T], dn[:, f, n * P:n * P + P], hT[:, f], start=(f == 0), stop=(f == FC - 1))
                        ins.then_inc(dn_used, 1)
                pe.wait_ge(stat_in, 2)
                column_sums(acc)
                pe.wait_ge(stat_in, 3)
                column_sums(sq)


def kernel(x_prompt, x_sample, state_conv, state_ssm_re, state_ssm_im,
           w_in, b_in, conv_w, w_conv_out, a_re, a_im, log_dt,
           ssm_b_re, ssm_b_im, ssm_c_re, ssm_c_im, ssm_d, w_glu, b_glu, w_ssm_out, w_o,
           ln1_g, ln1_b, w_router, router_bias, w_gate, w_up, w_down,
           ws_gate, ws_up, ws_down, ln2_g, ln2_b):
    import concourse.bacc as bacc
    from concourse.bass_utils import run_bass_kernel_spmd

    def a(x):
        return np.asarray(x)

    def chunks(v):
        return np.moveaxis(a(v).reshape(v.shape[:-1] + (KC, P)), -1, 0)

    def strips(w):
        return a(w).reshape(KC, P, -1, P).transpose(2, 1, 0, 3)

    def by_state(v):
        v = a(v).reshape(v.shape[:-2] + (NT, P))
        return np.moveaxis(v, -1, 0)

    f32 = np.float32
    x = np.concatenate([a(x_prompt)[0], a(x_sample)[:, 0]], axis=0)
    secs = strips(w_in[0]).reshape(6, KC, P, KC, P)
    order = [3, 1, 2, 0, 4, 5]
    w_front = np.concatenate([secs[i] for i in order] + [strips(w[0]) for w in (w_glu, w_conv_out, w_ssm_out, w_o)], axis=0)
    bin_ = chunks(a(b_in)[0].reshape(6, D)[order])
    dt = np.repeat(a(log_dt)[0][:, None], N, axis=1)
    rb = np.repeat(a(router_bias)[0][None, :], P, axis=0)
    vecs = np.concatenate([bin_.reshape(P, -1), chunks(b_glu[0]), chunks(conv_w[0]).reshape(P, -1), chunks(ssm_d[0]),
                           chunks(ln1_g[0]), chunks(ln1_b[0]), chunks(ln2_g[0]), chunks(ln2_b[0]),
                           by_state(a_re[0]), by_state(a_im[0]), by_state(dt), rb], axis=1)
    b_sm = np.zeros((P, 2, NT, 32), f32)
    c_sm = np.zeros((P, 2, NT, 32), f32)
    for r, (b, c) in enumerate(((ssm_b_re, ssm_c_re), (ssm_b_im, ssm_c_im))):
        b = a(b)[0].reshape(NT, 2, N, H)
        c = a(c)[0].reshape(NT, 2, H, N)
        for g in range(2):
            b_sm[g * N:g * N + N, r, :, g * H:g * H + H] = b[:, g].transpose(1, 0, 2)
            c_sm[g * N:g * N + N, r, :, g * H:g * H + H] = c[:, g].transpose(2, 0, 1)
    h0 = np.stack([by_state(state_ssm_re[0]), by_state(state_ssm_im[0])], axis=1).transpose(0, 1, 3, 2)
    cs = chunks(state_conv[0]).transpose(0, 3, 2, 1)

    def experts_in(g, u, n):
        w = np.concatenate([a(g).reshape(n, KC, P, F), a(u).reshape(n, KC, P, F)], axis=3)
        return w.transpose(0, 2, 1, 3).reshape(n, P, KC * 2 * F)

    def experts_out(w, n):
        return a(w).reshape(n, FC, P, D).transpose(0, 2, 1, 3).reshape(n, P, FC * D)

    arrays = {
        "x_t": x.T.reshape(KC, P, T).transpose(1, 0, 2),
        "w_front": w_front.reshape(-1, P, KC * P),
        "vecs": vecs,
        "b_sm": b_sm,
        "c_sm": c_sm,
        "h0": h0,
        "conv_state": cs,
        "w_router": a(w_router)[0].reshape(KC, P, E).transpose(1, 0, 2),
        "w_gu": np.concatenate([experts_in(w_gate[0], w_up[0], E), experts_in(ws_gate[0], ws_up[0], 1)], axis=0),
        "w_dn": np.concatenate([experts_out(w_down[0], E), experts_out(ws_down[0], 1)], axis=0),
    }
    outs = {"o_y": (P, KC, T), "o_conv_p": (P, KC, 2), "o_conv_s": (P, KC, 2, NS), "o_ssm_p": (P, 2, NT), "o_ssm_s": (P, 2, NT, NS)}
    nc = bacc.Bacc("TRN2", target_bir_lowering=False, num_devices=1)
    args = {}
    for name in arrays:
        arrays[name] = np.ascontiguousarray(arrays[name])
        args[name] = nc.dram_tensor(name, arrays[name].shape, F32, kind="ExternalInput").ap()
    for name, shape in outs.items():
        args[name] = nc.dram_tensor(name, shape, F32, kind="ExternalOutput").ap()
    build(nc, **args)
    res = run_bass_kernel_spmd(nc, [arrays], core_ids=[0]).results[0]

    y = res["o_y"].transpose(1, 0, 2).reshape(D, T).T
    conv_p = res["o_conv_p"].transpose(2, 1, 0).reshape(1, 1, 2, D)
    conv_s = res["o_conv_s"].transpose(3, 2, 1, 0).reshape(1, NS, 2, D)
    ssm_p = res["o_ssm_p"].transpose(1, 2, 0).reshape(2, 1, 1, G, N)
    ssm_s = res["o_ssm_s"].transpose(1, 3, 2, 0).reshape(2, 1, NS, G, N)
    c = np.ascontiguousarray
    return (c(y[:LP].reshape(1, LP, D)), c(y[LP:].reshape(NS, 1, D)), c(conv_p), c(ssm_p[0]), c(ssm_p[1]),
            c(conv_s), c(ssm_s[0]), c(ssm_s[1]))
```

```python
from contextlib import ExitStack

import numpy as np

import concourse.bass as bass
from concourse import mybir

ALU = mybir.AluOpType
ACT = mybir.ActivationFunctionType
AX = mybir.AxisListType
F32 = mybir.dt.float32
I32 = mybir.dt.int32

P = 128
D = 1024
KC = D // P
LP = 256
NS = 8
T = LP + NS
G, H, N = 64, 16, 64
NT = G * N // P
PB = P // 32
SEG = 64
NSEG = LP // SEG
HT = NT // 2
HC = KC // 2
E = 64
F = 256
FC = F // P
TOPK, RG, TOPG = 8, 8, 4
EG = E // RG
ROUTED_SCALE = 2.5
EPS = 1e-5
ALPHA = 2.0 ** 0.25
TC = 3

US, CG, XC, BG, GA, GB = range(6)
LOOP_STRIPS = 5 * KC
PER_SEG = LOOP_STRIPS // NSEG
RING = 8

V_BIN = 0
V_BGLU = V_BIN + 6 * KC
V_CW = V_BGLU + KC
V_D = V_CW + 3 * KC
V_LN = V_D + KC
V_ARE = V_LN + 4 * KC
V_AIM = V_ARE + NT
V_LDT = V_AIM + NT
V_RB = V_LDT + NT
NV = V_RB + E

EXP_C = [1.0 / 5040, 1.0 / 720, 1.0 / 120, 1.0 / 24, 1.0 / 6, 0.5, 1.0, 1.0]
LN2_HI, LN2_LO = 0.693359375, -2.12194440e-4
PI2_A, PI2_B, PI2_C = 6.28125, 1.9350051879882812e-03, 3.0199159819567e-07
MAGIC = 12582912.0
GONE = -1e30


class Steps:

    def __init__(self, eng, sem):
        self.eng, self.sem, self.n = eng, sem, 0

    def did(self, ins):
        ins.then_inc(self.sem, 1)
        self.n += 1
        return self.n

    def settle(self):
        self.eng.wait_ge(self.sem, self.n)


def build(nc, x_t, w_front, vecs, b_sm, c_sm, h0, conv_state, w_router, w_gu, ln2_rows, w_dn,
          o_y, o_conv_p, o_conv_s, o_ssm_p, o_ssm_s):
    with ExitStack() as ctx:
        def sb(name, shape, dt=F32):
            return ctx.enter_context(nc.sbuf_tensor(name, shape, dt))

        def sem(name):
            return ctx.enter_context(nc.semaphore(name))

        ring = sb("ring", [P, RING, KC, P])
        vec = sb("vec", [P, NV])
        ident = sb("ident", [P, P])
        ones = sb("ones", [P, P])
        xT = sb("xT", [P, KC, T])
        us = sb("us", [P, KC, T])
        proj = sb("proj", [P, 5 * KC, T])
        ys = sb("ys", [P, KC, T])
        cgb, xcb, bgb, gab, gbb = (proj[:, i * KC:(i + 1) * KC, :] for i in range(5))
        cst = sb("cst", [P, KC, 2, NS])
        sml = sb("sml", [P, 24, NT])

        psum = ctx.enter_context(nc.psum_tensor("banks", [P, 8, 512], F32))

        s_vec, s_x, s_bc, s_h0, s_cst = (sem(n) for n in ("vec_loaded", "x_loaded", "bc_loaded", "h0_loaded", "cst_loaded"))
        slot_loaded = [sem(f"slot{i}_loaded") for i in range(RING)]
        strips_done = sem("strips_done")
        bank_free = [sem(f"bank{i}_free") for i in range(2)]
        ident_ready = sem("ident_ready")
        before_ready = sem("before_ready")
        scores_cleared = sem("scores_cleared")
        pool_own = sem("pool_own")
        dve_own = sem("dve_own")
        dve_loop = sem("dve_loop")
        angles_ready = sem("angles_ready")
        sines_ready = sem("sines_ready")
        bb_ready = sem("bb_ready")
        bt_turned = sem("bt_turned")
        bt_ready = sem("bt_ready")
        tables_ready = sem("tables_ready")
        negc_ready = sem("negc_ready")
        seg_copied = sem("seg_copied")
        bx_ready = sem("bx_ready")
        demod_done = sem("demod_done")
        xt_ready = sem("xt_ready")
        scan_done = sem("scan_done")
        rot_done = sem("rot_done")
        h_ready = sem("h_ready")
        cy_ready = sem("cy_ready")
        y_evac = sem("y_evac")
        sx_ready = sem("sx_ready")
        sh_ready = sem("sh_ready")
        sy_ready = sem("sy_ready")
        s_fin_ready = sem("final_states_ready")
        ys_ready = sem("ys_ready")
        z_ready = sem("z_ready")
        gates_ready = sem("gates_ready")
        v_ready = sem("v_ready")
        u_ready = sem("u_ready")
        glu_ready = sem("glu_ready")
        m_ready = sem("m_ready")
        stat_in = sem("stat_in")
        stat_out = sem("stat_out")
        var_ready = sem("var_ready")
        std_ready = sem("std_ready")
        x1_ready = sem("x1_ready")
        logits_ready = sem("logits_ready")
        scores_ready = sem("scores_ready")
        comb_ready = sem("comb_ready")
        router_loaded = sem("router_loaded")
        xrow_turned = sem("xrow_turned")
        xrow_ready = sem("xrow_ready")
        rows_stored = sem("rows_stored")
        picks_ready = sem("picks_ready")
        counted = sem("counted")
        lists_ready = sem("lists_ready")
        iotas_ready = sem("iotas_ready")
        gathers_cleared = sem("gathers_cleared")
        shared_gu = sem("shared_gu")
        shared_silu = sem("shared_silu")
        shared_h = sem("shared_h")
        shared_dn = sem("shared_dn")
        shared_used = sem("shared_used")
        gu_in = [sem(f"gu_slot{i}_loaded") for i in range(4)]
        dn_in = [sem(f"dn_slot{i}_loaded") for i in range(4)]
        dve_idx = sem("dve_idx")
        eights_ready = sem("eights_ready")
        shifted = sem("positions_shifted")
        select_ready = sem("select_ready")
        selected = sem("selected")
        idx_ready = sem("idx_ready")
        gathered = [sem(f"gathered{i}") for i in range(2)]
        scattered = [sem(f"scattered{i}") for i in range(2)]
        turned = sem("turned")
        xg_ready = sem("xg_ready")
        gu_done = sem("gu_done")
        silu_done = sem("silu_done")
        hx_ready = sem("hx_ready")
        dn_done = sem("dn_done")
        y_scaled = sem("y_scaled")
        y_back = [sem(f"y_back{i}") for i in range(TC)]
        ln2_loaded = sem("ln2_loaded")
        tail_summed = sem("tail_summed")
        pool_summed = sem("pool_summed")
        var2_ready = sem("var2_ready")
        std2_ready = sem("std2_ready")
        rows_moved = sem("rows_moved")
        h_turned = sem("h_turned")
        hT_ready = sem("hT_ready")
        w_ready = sem("w_ready")
        moved = sem("moved")
        y_stored = sem("y_stored")
        y_ready = sem("y_ready")
        stored = sem("stored")

        with ExitStack() as fctx:
            def fsb(name, shape, dt=F32):
                return fctx.enter_context(nc.sbuf_tensor(name, shape, dt))

            cosT = fsb("cosT", [P, NT, SEG])
            sinT = fsb("sinT", [P, NT, SEG])
            decay = fsb("decay", [P, NT, SEG])
            prod = fsb("prod", [P, 4, HT, SEG])
            xt = fsb("xt", [P, 2, HT, SEG])
            gg = fsb("gg", [P, 2, HT, SEG])
            hh = fsb("hh", [P, 2, 2, HT, SEG])
            bT = fsb("bT", [P, 2, KC, P])
            cS = fsb("cS", [P, 2, NT, 32])
            seg_u = fsb("seg_u", [P, KC, SEG])
            h0s = fsb("h0s", [P, 2, NT, NS])
            b_in_sm = hh[:, 0].rearrange("p r t s -> p (r t s)").rearrange("p (r t c) -> p r t c", r=2, c=32)
            bb = hh[:, 1].rearrange("p r t s -> p (r t s)").rearrange("p (r t c) -> p r t c", r=2, c=32)
            hs = hh[:, 0].rearrange("p r t s -> p r (t s)")[:, :, 0:NT * NS].rearrange("p r (t b) -> p r t b", b=NS)

            bx = psum[:, 0:4, :].rearrange("p i (c r t) -> p i c r t", c=HC, r=2)

            def bx_half(r):
                return bx[:, :, :, r, :].rearrange("p i c t -> p c i t")

            def by_ci(ap):
                return ap.rearrange("p (c i) t -> p c i t", i=PB)

            with nc.Block() as block:

                @block.sync
                def _(sp):
                    sp.dma_start(vec[:], vecs).then_inc(s_vec, 16)
                    sp.dma_start(xT[:], x_t).then_inc(s_x, 16)
                    sp.dma_start(ring[:, 0], w_front[0]).then_inc(slot_loaded[0], 16)
                    sp.dma_start(b_in_sm, b_sm).then_inc(s_bc, 16)
                    sp.dma_start(cS[:], c_sm).then_inc(s_bc, 16)
                    for n in range(1, KC):
                        sp.dma_start(ring[:, n], w_front[n]).then_inc(slot_loaded[n], 16)
                    sp.dma_start(h0s[:], h0).then_inc(s_h0, 16)
                    sp.dma_start(cst[:], conv_state).then_inc(s_cst, 16)
                    with sp.Fori(0, NSEG) as g:
                        for j in range(PER_SEG):
                            n = g * PER_SEG + (KC + j)
                            sp.wait_ge(strips_done, n - 4)
                            sp.dma_start(ring[:, j % 5], w_front[bass.ds(n, 1)].rearrange("o p f -> (o p) f")).then_inc(slot_loaded[j % 5], 16)
                    for j in range(4):
                        sp.wait_ge(strips_done, 6 * KC + j - 3)
                        sp.dma_start(ring[:, j], w_front[6 * KC + j]).then_inc(slot_loaded[j], 16)
                    sp.wait_ge(s_fin_ready, 1)
                    sp.dma_start(o_ssm_p, sml[:, 18:20]).then_inc(stored, 16)
                    sp.wait_ge(sh_ready, 2)
                    sp.dma_start(o_ssm_s, hs).then_inc(stored, 16)
                    sp.wait_ge(stored, 32)

                @block.gpsimd
                def _(pool):
                    pool.sem_inc(h_ready, 1)
                    st = Steps(pool, pool_own)
                    st.did(pool.memset(ones[:], 1.0))
                    st.settle()
                    pool.affine_select(out=ident[:], in_=ones[:], pattern=[[-1, P]], compare_op=ALU.is_equal,
                                       fill=0.0, base=0, channel_multiplier=1).then_inc(ident_ready, 1)
                    pool.wait_ge(s_bc, 32)
                    pool.tensor_scalar(cS[:, 1], cS[:, 1], -1.0, None, ALU.mult).then_inc(negc_ready, 1)
                    with pool.Fori(0, NSEG) as g:
                        for half in range(2):
                            k = g * 2 + half
                            pool.wait_ge(demod_done, k + 2)
                            pool.wait_ge(scan_done, k + 1)
                            pool.tensor_tensor(xt[:, 0], prod[:, 0], prod[:, 1], ALU.add).then_inc(xt_ready, 1)
                            pool.tensor_tensor(xt[:, 1], prod[:, 2], prod[:, 3], ALU.subtract).then_inc(xt_ready, 1)
                            pool.wait_ge(rot_done, k + 1)
                            pool.wait_ge(cy_ready, k + 1)
                            pool.tensor_tensor(hh[:, half, 0], prod[:, 0], prod[:, 1], ALU.subtract).then_inc(h_ready, 1)
                            pool.tensor_tensor(hh[:, half, 1], prod[:, 2], prod[:, 3], ALU.add).then_inc(h_ready, 1)

                @block.scalar
                def _(act):
                    act.sem_inc(y_evac, 1)
                    act.wait_ge(s_vec, 16)
                    for n in range(KC):
                        act.wait_ge(strips_done, n + 1)
                        act.activation(us[:, n], psum[:, 5 + n % 2, 0:T], ACT.Identity,
                                       bias=vec[:, V_BIN + n:V_BIN + n + 1]).then_inc(bank_free[n % 2], 1)
                        if n == 0:
                            act.wait_ge(angles_ready, 1)
                            act.activation(sml[:, 8:10], sml[:, 8:10], ACT.Sin).then_inc(sines_ready, 1)
                    act.wait_ge(bank_free[0], KC // 2)
                    act.wait_ge(bank_free[1], KC // 2)
                    act.wait_ge(bt_turned, 1)
                    for r in range(2):
                        act.activation(bT[:, r].rearrange("p (a c) s -> p a (c s)", a=2), psum[:, 2 * r:2 * r + 2, :], ACT.Copy).then_inc(bt_ready, 1)
                    with act.Fori(0, NSEG) as g:
                        act.wait_ge(bx_ready, g * 2 + 1)
                        act.activation(seg_u[:], us[:, :, bass.ds(g * SEG, SEG)], ACT.Copy).then_inc(seg_copied, 1)
                        for half in range(2):
                            for j in range(5 * half, 5 * half + 5):
                                s = g * PER_SEG + j
                                act.wait_ge(strips_done, s + (KC + 1))
                                act.activation(proj[:, bass.ds(s, 1), :].rearrange("p o t -> p (o t)"), psum[:, 5 + j % 2, 0:T], ACT.Identity,
                                               bias=vec[:, bass.ds(s + (V_BIN + KC), 1)]).then_inc(bank_free[j % 2], 1)
                            act.wait_ge(cy_ready, g * 2 + (half + 2))
                            act.activation(ys[:, HC * half:HC * half + HC, bass.ds(g * SEG, SEG)],
                                           psum[:, 4, 0:HC * SEG].rearrange("p (c t) -> p c t", c=HC), ACT.Copy).then_inc(y_evac, 1)
                    act.wait_ge(sy_ready, 1)
                    act.activation(ys[:, :, LP:T], psum[:, 4, 0:KC * NS].rearrange("p (c t) -> p c t", c=KC), ACT.Copy).then_inc(y_evac, 1)

                @block.vector
                def _(dve):
                    dve.sem_inc(demod_done, 1)
                    dve.sem_inc(scan_done, 1)
                    st = Steps(dve, dve_own)

                    def do(ins):
                        st.did(ins)
                        st.settle()

                    V = vec
                    a_re, a_im, ldt = (V[:, c:c + NT] for c in (V_ARE, V_AIM, V_LDT))
                    S = [sml[:, i] for i in range(24)]
                    dt_, ard, aid, mag, lr, li, fr, fi = S[0:8]
                    sin_, cos_, t0, t1, t2, t3 = S[8:14]

                    def exp(out, x):
                        do(dve.tensor_scalar(t0, x, 1.4426950408889634, MAGIC, ALU.mult, ALU.add))
                        do(dve.tensor_scalar(t0, t0, -MAGIC, None, ALU.add))
                        do(dve.tensor_scalar(t0, t0, -126.0, 127.0, ALU.max, ALU.min))
                        do(dve.scalar_tensor_tensor(t1, t0, -LN2_HI, x, ALU.mult, ALU.add))
                        do(dve.scalar_tensor_tensor(t1, t0, -LN2_LO, t1, ALU.mult, ALU.add))
                        do(dve.tensor_scalar(t2, t1, EXP_C[0], None, ALU.mult))
                        for c in EXP_C[1:-1]:
                            do(dve.scalar_tensor_tensor(t2, t2, c, t1, ALU.add, ALU.mult))
                        do(dve.tensor_scalar(t3.bitcast(I32), t0, 127.0, 8388608.0, ALU.add, ALU.mult))
                        do(dve.scalar_tensor_tensor(out, t2, EXP_C[-1], t3, ALU.add, ALU.mult))

                    dve.wait_ge(s_vec, 16)
                    exp(dt_, ldt)
                    do(dve.tensor_tensor(ard, a_re, dt_, ALU.mult))
                    do(dve.tensor_tensor(aid, a_im, dt_, ALU.mult))
                    do(dve.tensor_scalar(t0, aid, 0.15915494309189535, MAGIC, ALU.mult, ALU.add))
                    do(dve.tensor_scalar(t0, t0, -MAGIC, None, ALU.add))
                    do(dve.scalar_tensor_tensor(t1, t0, -PI2_A, aid, ALU.mult, ALU.add))
                    do(dve.scalar_tensor_tensor(t1, t0, -PI2_B, t1, ALU.mult, ALU.add))
                    do(dve.scalar_tensor_tensor(t1, t0, -PI2_C, t1, ALU.mult, ALU.add))
                    do(dve.tensor_scalar(sin_, t1, 3.1415925, -3.1415925, ALU.min, ALU.max))
                    do(dve.scalar_tensor_tensor(t2, sin_, -1.0, sin_, ALU.mult, ALU.max))
                    st.did(dve.tensor_scalar(cos_, t2, -1.0, 1.5707963267948966, ALU.mult, ALU.add))
                    st.settle()
                    dve.sem_inc(angles_ready, 1)
                    exp(mag, ard)
                    dve.wait_ge(sines_ready, 1)
                    do(dve.tensor_tensor(lr, mag, cos_, ALU.mult))
                    do(dve.tensor_tensor(li, mag, sin_, ALU.mult))
                    do(dve.tensor_tensor(t0, a_re, a_re, ALU.mult))
                    do(dve.tensor_tensor(t1, a_im, a_im, ALU.mult))
                    do(dve.tensor_tensor(t0, t0, t1, ALU.add))
                    do(dve.reciprocal(t0, t0))
                    do(dve.tensor_scalar(t1, lr, -1.0, None, ALU.add))
                    do(dve.tensor_tensor(t2, t1, a_re, ALU.mult))
                    do(dve.tensor_tensor(t3, li, a_im, ALU.mult))
                    do(dve.tensor_tensor(t2, t2, t3, ALU.add))
                    do(dve.tensor_tensor(fr, t2, t0, ALU.mult))
                    do(dve.tensor_tensor(t2, li, a_re, ALU.mult))
                    do(dve.tensor_tensor(t3, t1, a_im, ALU.mult))
                    do(dve.tensor_tensor(t2, t2, t3, ALU.subtract))
                    do(dve.tensor_tensor(fi, t2, t0, ALU.mult))

                    def wide(v, m):
                        return v.rearrange("p (t o) -> p t o", o=1).broadcast_to([P, NT, m])

                    dve.wait_ge(s_bc, 32)
                    tmp = prod[:, 0].rearrange("p t s -> p (t s)").rearrange("p (t c) -> p t c", c=32)
                    frw, fiw = wide(fr, 32), wide(fi, 32)
                    do(dve.tensor_tensor(tmp, b_in_sm[:, 1], fiw, ALU.mult))
                    do(dve.tensor_tensor(bb[:, 0], b_in_sm[:, 0], frw, ALU.mult))
                    do(dve.tensor_tensor(bb[:, 0], bb[:, 0], tmp, ALU.subtract))
                    do(dve.tensor_tensor(tmp, b_in_sm[:, 0], fiw, ALU.mult))
                    do(dve.tensor_tensor(bb[:, 1], b_in_sm[:, 1], frw, ALU.mult))
                    dve.tensor_tensor(bb[:, 1], bb[:, 1], tmp, ALU.add).then_inc(bb_ready, 1)

                    do(dve.memset(cosT[:, :, 0:1], 1.0))
                    do(dve.memset(sinT[:, :, 0:1], 0.0))
                    vc, vs, wc, ws = cos_, sin_, S[14], S[15]
                    m = 1
                    while m < SEG:
                        c0, s0 = cosT[:, :, 0:m], sinT[:, :, 0:m]
                        c1, s1 = cosT[:, :, m:2 * m], sinT[:, :, m:2 * m]
                        pa = prod[:, 0:2].rearrange("p a t s -> p (a t) s")[:, :, 0:m]
                        pb = prod[:, 2:4].rearrange("p a t s -> p (a t) s")[:, :, 0:m]
                        st.did(dve.tensor_tensor(c1, c0, wide(vc, m), ALU.mult))
                        st.did(dve.tensor_tensor(pa, s0, wide(vs, m), ALU.mult))
                        st.did(dve.tensor_tensor(s1, s0, wide(vc, m), ALU.mult))
                        do(dve.tensor_tensor(pb, c0, wide(vs, m), ALU.mult))
                        st.did(dve.tensor_tensor(c1, c1, pa, ALU.subtract))
                        st.did(dve.tensor_tensor(s1, s1, pb, ALU.add))
                        st.did(dve.tensor_tensor(t0, vc, vc, ALU.mult))
                        st.did(dve.tensor_tensor(t1, vs, vs, ALU.mult))
                        do(dve.tensor_tensor(t2, vc, vs, ALU.mult))
                        st.did(dve.tensor_tensor(wc, t0, t1, ALU.subtract))
                        do(dve.tensor_scalar(ws, t2, 2.0, None, ALU.mult))
                        vc, vs, wc, ws = wc, ws, (S[16] if wc is S[14] else S[14]), (S[17] if ws is S[15] else S[15])
                        m *= 2
                    do(dve.tensor_copy(decay[:], wide(mag, SEG)))
                    dve.memset(decay[:, :, 0:1], 0.0).then_inc(tables_ready, 1)
                    dve.wait_ge(tables_ready, 1)

                    dve.wait_ge(bt_turned, 1)
                    for half in range(2):
                        do(dve.memset(hh[:, half, :, :, SEG - 1:SEG], 0.0))
                    with dve.Fori(0, NSEG) as g:
                        for half in range(2):
                            k = g * 2 + half
                            tiles = slice(HT * half, HT * half + HT)
                            ct, sn = by_ci(cosT[:, tiles]), by_ci(sinT[:, tiles])
                            dve.wait_ge(bx_ready, k + 2)
                            dve.wait_ge(h_ready, k * 2 + 1)
                            dve.tensor_tensor(by_ci(prod[:, 0]), bx_half(0), ct, ALU.mult)
                            dve.tensor_tensor(by_ci(prod[:, 1]), bx_half(1), sn, ALU.mult)
                            dve.tensor_tensor(by_ci(prod[:, 2]), bx_half(1), ct, ALU.mult)
                            dve.tensor_tensor(by_ci(prod[:, 3]), bx_half(0), sn, ALU.mult).then_inc(demod_done, 1)
                            base = g * (2 * 6) + 6 * half
                            c = sml[:, 18:22, 0:HT]
                            hr, hi = hh[:, half, 0, :, SEG - 1], hh[:, half, 1, :, SEG - 1]
                            lrh, lih = lr[:, tiles], li[:, tiles]
                            first = [xt[:, 0, :, 0], xt[:, 1, :, 0]]
                            dve.tensor_tensor(c[:, 0], lrh, hr, ALU.mult).then_inc(dve_loop, 1)
                            dve.tensor_tensor(c[:, 1], lih, hi, ALU.mult).then_inc(dve_loop, 1)
                            dve.tensor_tensor(c[:, 2], lrh, hi, ALU.mult).then_inc(dve_loop, 1)
                            dve.tensor_tensor(c[:, 3], lih, hr, ALU.mult).then_inc(dve_loop, 1)
                            dve.wait_ge(dve_loop, base + 4)
                            dve.tensor_tensor(c[:, 0], c[:, 0], c[:, 1], ALU.subtract).then_inc(dve_loop, 1)
                            dve.tensor_tensor(c[:, 2], c[:, 2], c[:, 3], ALU.add).then_inc(dve_loop, 1)
                            dve.wait_ge(dve_loop, base + 6)
                            dve.wait_ge(xt_ready, k * 2 + 2)
                            dve.tensor_tensor(first[0], first[0], c[:, 0], ALU.add).then_inc(sx_ready, 1)
                            dve.tensor_tensor(first[1], first[1], c[:, 2], ALU.add).then_inc(sx_ready, 1)
                            dve.wait_ge(sx_ready, k * 2 + 2)
                            dec = decay[:, tiles].rearrange("p t s -> p (t s)")
                            for r in range(2):
                                ins = dve.tensor_tensor_scan(gg[:, r].rearrange("p t s -> p (t s)"), dec,
                                                             xt[:, r].rearrange("p t s -> p (t s)"), 0.0, ALU.mult, ALU.add)
                            ins.then_inc(scan_done, 1)
                            dve.wait_ge(scan_done, k + 2)
                            ct, sn = cosT[:, tiles], sinT[:, tiles]
                            dve.tensor_tensor(prod[:, 0], gg[:, 0], ct, ALU.mult)
                            dve.tensor_tensor(prod[:, 1], gg[:, 1], sn, ALU.mult)
                            dve.tensor_tensor(prod[:, 2], gg[:, 1], ct, ALU.mult)
                            dve.tensor_tensor(prod[:, 3], gg[:, 0], sn, ALU.mult).then_inc(rot_done, 1)
                    fin = sml[:, 18:20]
                    dve.wait_ge(h_ready, 4 * NSEG + 1)
                    for r in range(2):
                        for half in range(2):
                            do(dve.tensor_copy(fin[:, r, half * HT:half * HT + HT], hh[:, half, r, :, SEG - 1]))
                    dve.sem_inc(s_fin_ready, 1)
                    dve.wait_ge(s_h0, 16)
                    dve.wait_ge(cy_ready, 2 * NSEG + 1)
                    q = [prod[:, i].rearrange("p t s -> p (t s)")[:, 0:NT * NS].rearrange("p (t b) -> p t b", b=NS) for i in range(4)]
                    do(dve.tensor_tensor(q[0], h0s[:, 0], wide(lr, NS), ALU.mult))
                    do(dve.tensor_tensor(q[1], h0s[:, 1], wide(li, NS), ALU.mult))
                    do(dve.tensor_tensor(q[2], h0s[:, 1], wide(lr, NS), ALU.mult))
                    do(dve.tensor_tensor(q[3], h0s[:, 0], wide(li, NS), ALU.mult))
                    do(dve.tensor_tensor(q[0], q[0], q[1], ALU.subtract))
                    do(dve.tensor_tensor(q[2], q[2], q[3], ALU.add))
                    dve.wait_ge(bx_ready, 2 * NSEG + 2)
                    sx = psum[:, 0:4, 0:2 * KC * NS].rearrange("p i (c r b) -> p i c r b", c=KC, r=2)
                    for r in range(2):
                        dve.tensor_tensor(by_ci(hs[:, r]), sx[:, :, :, r, :].rearrange("p i c b -> p c i b"),
                                          by_ci(q[2 * r]), ALU.add).then_inc(sh_ready, 1)

                @block.tensor
                def _(pe):
                    def strip(slot, loads, n2, par, rhs):
                        pe.wait_ge(slot_loaded[slot], loads)
                        pe.wait_ge(bank_free[par], n2)
                        for k in range(KC):
                            ins = pe.matmul(psum[:, 5 + par, 0:T], ring[:, slot, k], rhs[:, k], start=(k == 0), stop=(k == KC - 1))
                        ins.then_inc(strips_done, 1)

                    pe.sem_inc(cy_ready, 1)
                    pe.sem_inc(bx_ready, 1)
                    pe.wait_ge(s_x, 16)
                    for n in range(KC):
                        pe.wait_ge(slot_loaded[n], 16)
                        if n >= 2:
                            pe.wait_ge(bank_free[n % 2], n // 2)
                        for k in range(KC):
                            ins = pe.matmul(psum[:, 5 + n % 2, 0:T], ring[:, n, k], xT[:, k], start=(k == 0), stop=(k == KC - 1))
                        ins.then_inc(strips_done, 1)
                    pe.wait_ge(ident_ready, 1)
                    pe.wait_ge(bb_ready, 1)
                    for r in range(2):
                        for c in range(KC):
                            ins = pe.transpose(psum[:, 2 * r + c // 4, (c % 4) * P:(c % 4) * P + P],
                                               bb[:, r, PB * c:PB * c + PB].rearrange("p t c -> p (t c)"), ident[:])
                    ins.then_inc(bt_turned, 1)
                    pe.wait_ge(bt_ready, 2)
                    pe.wait_ge(negc_ready, 1)
                    pe.wait_ge(bank_free[0], KC // 2)
                    pe.wait_ge(bank_free[1], KC // 2)
                    with pe.Fori(0, NSEG) as g:
                        for half in range(2):
                            k = g * 2 + half
                            if half == 0:
                                pe.wait_ge(seg_copied, g + 1)
                            pe.wait_ge(demod_done, k + 1)
                            for c in range(HC):
                                for i in range(PB):
                                    rows = slice(32 * i, 32 * i + 32)
                                    for r in range(2):
                                        ins = pe.matmul(bx[:, i, c, r, :], bT[rows, r, HC * half + c, :], seg_u[rows, HC * half + c, :],
                                                        start=True, stop=True)
                            ins.then_inc(bx_ready, 1)
                            for j in range(5 * half, 5 * half + 5):
                                n2 = g * 5 + (4 + j // 2)
                                strip(j % 5, g * 32 + (32 + 16 * (j // 5)), n2, j % 2, xT)
                            pe.wait_ge(h_ready, k * 2 + 3)
                            pe.wait_ge(y_evac, k + 1)
                            for c in range(HC):
                                for i in range(PB):
                                    t = PB * c + i
                                    for r in range(2):
                                        ins = pe.matmul(psum[32 * i:32 * i + 32, 4, SEG * c:SEG * c + SEG], cS[:, r, HT * half + t],
                                                        hh[:, half, r, t], start=(r == 0), stop=(r == 1))
                            ins.then_inc(cy_ready, 1)
                    pe.wait_ge(demod_done, 2 * NSEG + 1)
                    sx = psum[:, 0:4, 0:2 * KC * NS].rearrange("p i (c r b) -> p i c r b", c=KC, r=2)
                    for c in range(KC):
                        for i in range(PB):
                            rows = slice(32 * i, 32 * i + 32)
                            for r in range(2):
                                ins = pe.matmul(sx[:, i, c, r, :], bT[rows, r, c, :], us[rows, c, LP:T], start=True, stop=True)
                    ins.then_inc(bx_ready, 1)
                    pe.wait_ge(sh_ready, 2)
                    pe.wait_ge(y_evac, 2 * NSEG + 1)
                    for c in range(KC):
                        for i in range(PB):
                            for r in range(2):
                                ins = pe.matmul(psum[32 * i:32 * i + 32, 4, NS * c:NS * c + NS], cS[:, r, PB * c + i], hs[:, r, PB * c + i],
                                                start=(r == 0), stop=(r == 1))
                    ins.then_inc(sy_ready, 1)
        SL = 64
        SLOTS = 4
        PAIRS = E // 2
        BIG = float(1 << 20)
        gu = sb("gu", [P, SLOTS, KC, 2 * F])
        dn = sb("dn", [P, SLOTS, FC, D])
        wr = sb("wr", [P, KC, E])
        tri = sb("tri", [P, P])
        eights = sb("eights", [P, NS])

        def carve(t, pattern, *shapes):
            flat, at, out = t.rearrange(pattern), 0, []
            for shape in shapes:
                n = int(np.prod(shape))
                names = "abcd"[:len(shape)]
                v = flat[:, at:at + n].rearrange(f"p ({' '.join(names)}) -> p {' '.join(names)}", **{m: k for m, k in zip(names, shape)})
                out.append(v)
                at += n
            assert at <= flat.shape[1], (at, flat.shape)
            return out

        x_rows, xg, y_rows, hT, sil, hT_sl, h_sl, sil_sl = carve(
            ring[:], "p s k m -> p (s k m)", (2, D), (2, KC, P), (2, D), (FC, T), (FC, T), (FC, 2 * SL), (F,), (F,))
        xrow, arow = carve(proj[:, 2 * KC:5 * KC], "p s t -> p (s t)", (TC, D), (TC, D))
        scores, rt, top8, cmp, before = carve(ys[:], "p k t -> p (k t)", (TC, E), (5, TC, E), (TC, RG, 8), (TC, RG, RG), (RG, RG))
        val, pos, S, iota, pk, small = carve(xT[:], "p k t -> p (k t)", (TC, E, 3), (TC, E), (2, TC, 2 * SL), (SL,), (TC, E), (64,))
        meta, dest, wnow, stats, mv = carve(sml[:], "p a t -> p (a t)", (2, 4), (2, 2), (2, 1), (TC, 2, 6), (TC, 4))
        rounds = sb("rounds", [P, 1], I32)
        idx = sb("idx", [P, 2, 2], mybir.dt.uint32)
        idx_y = sb("idx_y", [P, 2], mybir.dt.uint32)
        r_, x1, sq = xcb, cgb, us
        mu = sb("mu", [P, 3, T])
        tok = [P, P, NS]
        x_dram = nc.dram_tensor("x_rows_dram", [T, D], F32, kind="Internal").ap()
        y_dram = nc.dram_tensor("y_rows_dram", [T * TOPK, D], F32, kind="Internal").ap()
        tokid = small[:, 0:TC]
        tok8 = small[:, TC:2 * TC]

        with nc.Block() as block:

            def n_rounds(eng):
                eng.wait_ge(lists_ready, 1)
                return eng.value_load(rounds[0:1, 0:1], min_val=1, max_val=5)

            @block.sync
            def _(sp):
                sp.dma_start(wr[:], w_router).then_inc(router_loaded, 16)
                parts = [("gu", E, 3), ("dn", E, 3), ("gu", 0, 0), ("gu", 1, 1), ("dn", 0, 0), ("dn", 1, 1), ("gu", 2, 2)]
                for g in range(1, 8):
                    for j in range(4):
                        n = 6 * KC + 4 * g + j
                        sp.wait_ge(strips_done, n - 3)
                        sp.dma_start(ring[:, j], w_front[n]).then_inc(slot_loaded[j], 16)
                    kind, e, s = parts[g - 1]
                    if kind == "gu":
                        sp.dma_start(gu[:, s], w_gu[e]).then_inc(gu_in[s], 16)
                    else:
                        sp.dma_start(dn[:, s], w_dn[e]).then_inc(dn_in[s], 16)
                sp.dma_start(dn[:, 2], w_dn[2]).then_inc(dn_in[2], 16)
                sp.wait_ge(u_ready, 1)
                sp.dma_start(o_conv_p, cgb[:, :, LP - 2:LP]).then_inc(stored, 16)
                sp.dma_start(o_conv_s[:, :, 0], cst[:, :, 1]).then_inc(stored, 16)
                sp.dma_start(o_conv_s[:, :, 1], cgb[:, :, LP:T]).then_inc(stored, 16)
                for c in range(TC):
                    sp.wait_ge(xrow_ready, c + 1)
                    sp.dma_start(x_dram[c * P:c * P + tok[c]], xrow[0:tok[c], c]).then_inc(rows_stored, 16)
                sp.wait_ge(shared_gu, 2 * FC)
                sp.dma_start(gu[:, 3], w_gu[3]).then_inc(gu_in[3], 16)
                sp.wait_ge(shared_dn, TC)
                sp.dma_start(dn[:, 3], w_dn[3]).then_inc(dn_in[3], 16)
                R = n_rounds(sp)
                all_stored = sp.snap(R * (16 * PAIRS // 2))
                all_gathered = sp.snap(all_stored + 16)
                with sp.Fori(1, R * (PAIRS // 2)) as q:
                    for s in range(SLOTS):
                        e = (q * SLOTS + s) % E
                        sp.wait_ge(gu_done, q * 2 + (s // 2 - 1))
                        sp.dma_start(gu[:, s], w_gu[bass.ds(e, 1)].rearrange("o p f -> (o p) f")).then_inc(gu_in[s], 16)
                        sp.wait_ge(dn_done, q * 2 + (s // 2 - 1))
                        sp.dma_start(dn[:, s], w_dn[bass.ds(e, 1)].rearrange("o p f -> (o p) f")).then_inc(dn_in[s], 16)
                for u in range(2):
                    sp.wait_ge(gathered[u], all_gathered)
                for u in range(2):
                    sp.wait_ge(scattered[u], all_stored)
                by_tok = y_dram.rearrange("(t r) d -> t (r d)", r=TOPK)
                sp.dma_start(dn[:, 1], ln2_rows).then_inc(ln2_loaded, 16)
                for c in range(2):
                    sp.dma_start(gu[:, 2 * c:2 * c + 2].rearrange("p s k f -> p (s k f)"), by_tok[c * P:c * P + P]).then_inc(y_back[c], 16)
                sp.dma_start(dn[0:NS * TOPK, 0, 0], y_dram[2 * P * TOPK:T * TOPK]).then_inc(y_back[2], 16)
                for c in range(TC):
                    sp.wait_ge(y_ready, c + 1)
                    sp.dma_start(o_y[c * P:c * P + tok[c]], arow[0:tok[c], c]).then_inc(stored, 16)
                sp.wait_ge(stored, 16 * (5 + TC))

            @block.gpsimd
            def _(pool):
                pool.sem_inc(y_stored, 2)
                pool.affine_select(out=tri[:], in_=ones[:], pattern=[[1, P]], compare_op=ALU.is_gt,
                                   fill=0.0, base=0, channel_multiplier=-1).then_inc(before_ready, 1)
                pool.affine_select(out=eights[:], in_=ones[:, 0:NS], pattern=[[-TOPK, NS]], compare_op=ALU.is_ge,
                                   fill=0.0, base=0, channel_multiplier=1).then_inc(eights_ready, 1)
                pool.wait_ge(eights_ready, 1)
                pool.affine_select(out=eights[:], in_=eights[:], pattern=[[TOPK, NS]], compare_op=ALU.is_ge,
                                   fill=0.0, base=TOPK - 1, channel_multiplier=-1).then_inc(eights_ready, 1)
                pool.wait_ge(strips_done, 10 * KC)
                pool.affine_select(out=before, in_=ones[:, 0:RG * RG].rearrange("p (g h) -> p g h", g=RG), pattern=[[1, RG], [-1, RG]],
                                   compare_op=ALU.is_gt, fill=0.0, base=0, channel_multiplier=0).then_inc(before_ready, 1)
                pool.memset(x_rows, 0.0).then_inc(gathers_cleared, 1)
                for b in range(2):
                    pool.wait_ge(bank_free[b], 4 + 5 * NSEG + 16)
                pool.iota(iota, pattern=[[1, SL]], base=0, channel_multiplier=0, allow_small_or_imprecise_dtypes=True).then_inc(iotas_ready, 1)
                pool.iota(tokid, pattern=[[P, TC]], base=1, channel_multiplier=1, allow_small_or_imprecise_dtypes=True).then_inc(iotas_ready, 1)
                pool.iota(tok8, pattern=[[P * TOPK, TC]], base=1, channel_multiplier=TOPK, allow_small_or_imprecise_dtypes=True).then_inc(iotas_ready, 1)
                pool.wait_ge(rows_stored, 16 * TC)
                pool.wait_ge(gathers_cleared, 1)
                R = n_rounds(pool)

                last_x, last_y = pool.to_reg(T - 1), pool.to_reg(T * TOPK - 1)

                def gather(u):
                    pool.sem_inc(rows_moved, 1)
                    pool.indirect_dma_start(x_rows[:, u], None, x_dram, bass.IndirectOffsetOnAxis(ap=idx[:, u, 0:1], axis=0),
                                            bounds_check=last_x, oob_is_err=False).then_inc(gathered[u], 16)

                for u in range(2):
                    pool.wait_ge(idx_ready, u + 1)
                    gather(u)

                def step(u, q):
                    it = q * 2 + u
                    pool.wait_ge(idx_ready, it + 3)
                    pool.wait_ge(turned, it + 1)
                    gather(u)
                    if not (isinstance(q, int) and it == 0):
                        pool.wait_ge(scattered[1 - u], q * 16 + 16 * u)
                        pool.sem_inc(y_stored, 1)
                    pool.wait_ge(y_scaled, it + 2)
                    pool.sem_inc(rows_moved, 1)
                    pool.indirect_dma_start(y_dram, bass.IndirectOffsetOnAxis(ap=idx_y[:, u:u + 1], axis=0), y_rows[:, u], None,
                                            bounds_check=last_y, oob_is_err=False).then_inc(scattered[u], 16)

                for u in range(2):
                    step(u, 0)
                with pool.Fori(1, R * (PAIRS // 2)) as q:
                    for u in range(2):
                        step(u, q)
                pool.wait_ge(y_back[1], 16)
                back = gu[:, 2:4].rearrange("p s k f -> p (s k f)").rearrange("p (r d) -> p r d", r=TOPK)
                for r in range(TOPK):
                    pool.tensor_tensor(arow[:, 1], arow[:, 1], back[:, r], ALU.add).then_inc(pool_summed, 1)
                    pool.wait_ge(pool_summed, r + 1)

            @block.scalar
            def _(act):
                act.sem_inc(y_scaled, 1)
                act.wait_ge(ys_ready, 1)
                act.activation(ys[:], ys[:], ACT.Gelu_apprx_tanh).then_inc(z_ready, 1)
                act.wait_ge(bank_free[0], 4 + 5 * NSEG)
                act.wait_ge(bank_free[1], 4 + 5 * NSEG)
                act.activation(proj[:, 3 * KC:5 * KC], proj[:, 3 * KC:5 * KC], ACT.Sigmoid).then_inc(gates_ready, 1)
                for n in range(KC):
                    act.wait_ge(strips_done, 6 * KC + n + 1)
                    act.activation(us[:, n], psum[:, 5 + n % 2, 0:T], ACT.Sigmoid,
                                   bias=vec[:, V_BGLU + n:V_BGLU + n + 1]).then_inc(bank_free[n % 2], 1)

                act.wait_ge(var_ready, 1)
                act.activation(mu[:, 1], mu[:, 1], ACT.Sqrt).then_inc(std_ready, 1)
                act.wait_ge(scores_cleared, 1)
                act.wait_ge(logits_ready, TC)
                for c in range(TC):
                    act.activation(scores[0:tok[c], c], psum[0:tok[c], 7, c * E:c * E + E], ACT.Sigmoid).then_inc(scores_ready, 1)
                for c in range(TC):
                    act.wait_ge(xrow_turned, c + 1)
                    act.activation(xrow[0:tok[c], c], psum[0:tok[c], 2 * (c % 2):2 * (c % 2) + 2].rearrange("p b f -> p (b f)"), ACT.Copy).then_inc(xrow_ready, 1)
                act.wait_ge(shared_gu, 2 * FC)
                for f in range(FC):
                    act.activation(sil[:, f], psum[:, f, 0:T], ACT.Silu).then_inc(shared_silu, 1)
                R = n_rounds(act)

                def rows_in(u, it):
                    act.wait_ge(turned, it)
                    act.activation(xg[:, u].rearrange("p (b k) s -> p b (k s)", b=2), psum[:, 2:4], ACT.Copy).then_inc(xg_ready, 1)

                rows_in(0, 1)
                with act.Fori(0, R * (PAIRS // 2)) as q:
                    for u in range(2):
                        it = q * 2 + u
                        act.wait_ge(gu_done, it + 1)
                        act.wait_ge(hx_ready, it + 1)
                        act.activation(sil_sl, psum[:, u, 0:F], ACT.Silu).then_inc(silu_done, 1)
                        rows_in(1 - u, it + 2)
                        act.wait_ge(h_turned, it + 1)
                        act.activation(hT_sl.rearrange("p f s -> p (f s)"), psum[:, 7, 0:FC * 2 * SL], ACT.Copy).then_inc(hT_ready, 1)
                        act.wait_ge(dn_done, it + 1)
                        act.wait_ge(y_stored, it + 1)
                        act.wait_ge(w_ready, it + 1)
                        act.activation(y_rows[:, u], psum[:, 4:6].rearrange("p b f -> p (b f)"), ACT.Copy, scale=wnow[:, u]).then_inc(y_scaled, 1)
                act.wait_ge(var2_ready, 1)
                act.activation(mv[:, :, 3], mv[:, :, 2], ACT.Sqrt).then_inc(std2_ready, 1)

            @block.vector
            def _(dve):
                st = Steps(dve, dve_loop)
                st.n = 12 * NSEG
                V = vec
                dve.sem_inc(hx_ready, 1)

                def do(ins):
                    st.did(ins)
                    st.settle()

                dve.wait_ge(y_evac, 2 * NSEG + 2)
                for n in range(KC):
                    st.did(dve.scalar_tensor_tensor(ys[:, n], us[:, n], V[:, V_D + n:V_D + n + 1], ys[:, n], ALU.mult, ALU.add))
                st.settle()
                dve.sem_inc(ys_ready, 1)
                dve.wait_ge(bank_free[0], 4 + 5 * NSEG)
                dve.wait_ge(bank_free[1], 4 + 5 * NSEG)
                dve.wait_ge(s_cst, 16)
                do(dve.tensor_tensor(cgb, cgb, xcb, ALU.mult))
                dve.sem_inc(u_ready, 1)

                def cw(k, n):
                    return V[:, V_CW + k * KC + n:V_CW + k * KC + n + 1]

                for n in range(KC):
                    st.did(dve.tensor_scalar(xcb[:, n], cgb[:, n], cw(2, n), None, ALU.mult))
                st.settle()
                for n in range(KC):
                    st.did(dve.scalar_tensor_tensor(xcb[:, n, 1:LP], cgb[:, n, 0:LP - 1], cw(1, n), xcb[:, n, 1:LP], ALU.mult, ALU.add))
                    st.did(dve.scalar_tensor_tensor(xcb[:, n, LP:T], cst[:, n, 1], cw(1, n), xcb[:, n, LP:T], ALU.mult, ALU.add))
                st.settle()
                for n in range(KC):
                    st.did(dve.scalar_tensor_tensor(xcb[:, n, 2:LP], cgb[:, n, 0:LP - 2], cw(0, n), xcb[:, n, 2:LP], ALU.mult, ALU.add))
                    st.did(dve.scalar_tensor_tensor(xcb[:, n, LP:T], cst[:, n, 0], cw(0, n), xcb[:, n, LP:T], ALU.mult, ALU.add))
                st.settle()
                do(dve.tensor_tensor(xcb, xcb, bgb, ALU.mult))
                dve.sem_inc(v_ready, 1)
                for n in range(KC):
                    dve.wait_ge(bank_free[n % 2], 4 + 5 * NSEG + n // 2 + 1)
                    st.did(dve.tensor_tensor(us[:, n], ys[:, n], us[:, n], ALU.mult))
                st.settle()
                dve.sem_inc(glu_ready, 1)
                dve.wait_ge(gates_ready, 1)
                for n in range(KC):
                    dve.wait_ge(strips_done, 7 * KC + n + 1)
                    dve.tensor_tensor(bgb[:, n], psum[:, 5 + n % 2, 0:T], gab[:, n], ALU.mult).then_inc(bank_free[n % 2], 1)
                for n in range(KC):
                    dve.wait_ge(strips_done, 8 * KC + n + 1)
                    dve.tensor_tensor(gbb[:, n], psum[:, 5 + n % 2, 0:T], gbb[:, n], ALU.mult).then_inc(bank_free[n % 2], 1)
                    dve.wait_ge(bank_free[n % 2], 4 + 5 * NSEG + 4 + 4 + n // 2 + 1)
                    do(dve.tensor_tensor(ys[:, n], gbb[:, n], bgb[:, n], ALU.add))
                dve.sem_inc(m_ready, 1)
                for n in range(KC):
                    dve.wait_ge(strips_done, 9 * KC + n + 1)
                    dve.scalar_tensor_tensor(xcb[:, n], xT[:, n], ALPHA, psum[:, 5 + n % 2, 0:T], ALU.mult, ALU.add).then_inc(bank_free[n % 2], 1)

                wide = mu[:, 0:1].broadcast_to([P, KC, T])
                dve.wait_ge(stat_out, 1)
                do(dve.tensor_scalar(mu[:, 0], psum[:, 4, 0:T], 1.0 / D, None, ALU.mult))
                do(dve.tensor_tensor(r_, r_, wide, ALU.subtract))
                do(dve.tensor_tensor(sq[:], r_, r_, ALU.mult))
                dve.sem_inc(stat_in, 1)
                dve.wait_ge(stat_out, 2)
                do(dve.tensor_scalar(mu[:, 0], psum[:, 4, 0:T], 1.0 / D, EPS, ALU.mult, ALU.add))
                do(dve.reciprocal(mu[:, 1], mu[:, 0]))
                dve.sem_inc(var_ready, 1)
                dve.wait_ge(std_ready, 1)
                do(dve.tensor_tensor(mu[:, 2], mu[:, 1], mu[:, 1], ALU.mult))
                do(dve.tensor_tensor(mu[:, 2], mu[:, 2], mu[:, 0], ALU.mult))
                do(dve.tensor_scalar(mu[:, 2], mu[:, 2], -0.5, 1.5, ALU.mult, ALU.add))
                do(dve.tensor_tensor(mu[:, 0], mu[:, 2], mu[:, 1], ALU.mult))
                do(dve.tensor_tensor(r_, r_, wide, ALU.mult))
                dve.wait_ge(stored, 16 * 5)
                for n in range(KC):
                    st.did(dve.tensor_scalar(x1[:, n], r_[:, n], vec[:, V_LN + n:V_LN + n + 1], vec[:, V_LN + KC + n:V_LN + KC + n + 1], ALU.mult, ALU.add))
                st.settle()
                dve.sem_inc(x1_ready, 1)

                biased, masked, left, picked, wts = (rt[:, i] for i in range(5))
                gs, rank, cnt = (small[:, 6 + 8 * i:6 + 8 * i + 8] for i in range(3))
                total, cm, over = small[:, 30:33], small[:, 33:34], small[:, 34:38]
                dve.memset(scores, 0.5).then_inc(scores_cleared, 1)
                dve.wait_ge(iotas_ready, 3)
                do(dve.memset(pk, 0.0))
                dve.wait_ge(scores_ready, TC)
                rb = vec[:, V_RB:V_RB + E].rearrange("p (o e) -> p o e", o=1).broadcast_to([P, TC, E])
                do(dve.tensor_tensor(biased, scores, rb, ALU.add))
                for c in range(TC):
                    for g in range(RG):
                        st.did(dve.max(top8[:, c, g], biased[:, c, g * EG:g * EG + EG]))
                st.settle()
                dve.wait_ge(before_ready, 2)
                for c in range(TC):
                    do(dve.tensor_tensor(gs, top8[:, c, :, 0], top8[:, c, :, 1], ALU.add))
                    me = gs.rearrange("p (g o) -> p g o", o=1).broadcast_to([P, RG, RG])
                    other = gs.rearrange("p (o g) -> p o g", o=1).broadcast_to([P, RG, RG])
                    eq = cmp[:, c]
                    do(dve.tensor_tensor(eq, other, me, ALU.is_equal))
                    do(dve.tensor_tensor(eq, eq, before, ALU.mult))
                    do(dve.tensor_reduce(cnt, eq, AX.X, ALU.add))
                    do(dve.tensor_tensor(eq, other, me, ALU.is_gt))
                    do(dve.tensor_reduce(rank, eq, AX.X, ALU.add))
                    do(dve.tensor_tensor(rank, rank, cnt, ALU.add))
                    do(dve.tensor_scalar(rank, rank, float(TOPG), None, ALU.is_lt))
                    do(dve.tensor_scalar(rank, rank, -GONE, GONE, ALU.mult, ALU.add))
                    gm = rank.rearrange("p (g o) -> p g o", o=1).broadcast_to([P, RG, EG])
                    do(dve.tensor_tensor(masked[:, c].rearrange("p (g e) -> p g e", g=RG), biased[:, c].rearrange("p (g e) -> p g e", g=RG), gm, ALU.add))
                    do(dve.max(top8[:, c, 0], masked[:, c]))
                    do(dve.match_replace(left[:, c], top8[:, c, 0], masked[:, c], 3 * GONE))
                do(dve.tensor_tensor(picked, left, masked, ALU.not_equal))
                st.did(dve.tensor_copy(pk[:, 0:2], picked[:, 0:2]))
                st.did(dve.tensor_copy(pk[0:NS, 2], picked[0:NS, 2]))
                st.settle()
                dve.sem_inc(picks_ready, 1)
                do(dve.tensor_tensor(wts, scores, picked, ALU.mult))
                do(dve.tensor_reduce(total, wts, AX.X, ALU.add))
                do(dve.reciprocal(total, total))
                for c in range(TC):
                    st.did(dve.tensor_scalar(val[:, c, :, 0], wts[:, c], total[:, c:c + 1], ROUTED_SCALE, ALU.mult, ALU.mult))
                    st.did(dve.tensor_scalar(val[:, c, :, 1], pk[:, c], 0.0, tokid[:, c:c + 1], ALU.mult, ALU.add))
                    st.did(dve.tensor_tensor_scan(masked[:, c], ones[:, 0:E], pk[:, c], 0.0, ALU.mult, ALU.add))
                st.settle()
                do(dve.tensor_tensor(masked, masked, pk, ALU.subtract))
                for c in range(TC):
                    st.did(dve.tensor_scalar(val[:, c, :, 2], masked[:, c], tok8[:, c:c + 1], None, ALU.add))
                do(dve.tensor_scalar(left, pk, -1000.0, 1000.0, ALU.mult, ALU.add))
                dve.wait_ge(counted, 1)
                st.did(dve.tensor_tensor(pos, psum[:, 6, 0:TC * E].rearrange("p (c e) -> p c e", c=TC), left, ALU.add))
                do(dve.tensor_reduce(cm, psum[:, 6, TC * E:TC * E + E], AX.X, ALU.max))
                for i in range(4):
                    st.did(dve.tensor_scalar(over[:, i:i + 1], cm, float(SL * (i + 1)), None, ALU.is_gt))
                st.settle()
                do(dve.tensor_reduce(cm, over, AX.X, ALU.add))
                do(dve.tensor_scalar(rounds[:], cm, 1.0, None, ALU.add))
                dve.sem_inc(lists_ready, 1)
                R = n_rounds(dve)

                def select(u, pair, nth):
                    p2 = pos[:, :, bass.ds(pair * 2, 2)]
                    dve.tensor_tensor(S[:, u].rearrange("p c (j s) -> p c j s", j=2),
                                      iota.rearrange("p (c j s) -> p c j s", c=1, j=1).broadcast_to([P, TC, 2, SL]),
                                      p2.rearrange("p c (j s) -> p c j s", s=1).broadcast_to([P, TC, 2, SL]), ALU.is_equal).then_inc(select_ready, 1)
                    dve.wait_ge(select_ready, nth)
                    dve.tensor_scalar(p2, p2, -float(SL), None, ALU.add).then_inc(shifted, 1)

                def indices(u, base):
                    for j in range(2):
                        h = slice(SL * j, SL * j + SL)
                        dve.tensor_copy(meta[h, u, 0:3], psum[h, 6, 3 * j:3 * j + 3]).then_inc(dve_idx, 1)
                    dve.wait_ge(dve_idx, base + 2)
                    dve.tensor_scalar(dest[:, u], meta[:, u, 1:3], 0.0, BIG, ALU.is_equal, ALU.mult).then_inc(dve_idx, 1)
                    dve.wait_ge(dve_idx, base + 3)
                    dve.scalar_tensor_tensor(idx[:, u], meta[:, u, 1:3], -1.0, dest[:, u], ALU.add, ALU.add).then_inc(idx_ready, 1)

                for u in range(2):
                    select(u, u, u + 1)
                    dve.wait_ge(selected, u + 1)
                    indices(u, 3 * u)
                for f in range(FC):
                    dve.wait_ge(shared_silu, f + 1)
                    dve.tensor_tensor(hT[:, f], sil[:, f], psum[:, FC + f, 0:T], ALU.mult).then_inc(shared_h, 1)
                for c in range(TC):
                    t = slice(0, tok[c])
                    dve.wait_ge(xrow_ready, c + 1)
                    dve.wait_ge(shared_dn, c + 1)
                    dve.scalar_tensor_tensor(arow[t, c], xrow[t, c], ALPHA, psum[t, 4:6].rearrange("p b f -> p (b f)"), ALU.mult, ALU.add).then_inc(shared_used, 1)
                with dve.Fori(0, R * (PAIRS // 2)) as q:
                    for u in range(2):
                        it = q * 2 + u
                        dve.wait_ge(y_stored, it + 1)
                        dve.wait_ge(idx_ready, it + 1)
                        dve.tensor_copy(wnow[:, u], meta[:, u, 0:1]).then_inc(w_ready, 1)
                        dve.tensor_copy(idx_y[:, u:u + 1], idx[:, u, 1:2]).then_inc(moved, 1)
                        dve.wait_ge(selected, it + 1)
                        dve.wait_ge(shifted, it + 2)
                        select(u, (it + 2) % PAIRS, it + 3)
                        dve.wait_ge(silu_done, it + 1)
                        dve.tensor_tensor(h_sl, sil_sl, psum[:, u, F:2 * F], ALU.mult).then_inc(hx_ready, 1)
                        dve.wait_ge(selected, it + 3)
                        dve.wait_ge(turned, it + 1)
                        dve.wait_ge(w_ready, it + 1)
                        dve.wait_ge(moved, it + 1)
                        indices(u, it * 3 + 6)
                back = gu[:, 0:2].rearrange("p s k f -> p (s k f)").rearrange("p (r d) -> p r d", r=TOPK)
                dve.wait_ge(shared_used, TC)
                dve.wait_ge(y_back[0], 16)
                for r in range(TOPK):
                    do(dve.tensor_tensor(arow[:, 0], arow[:, 0], back[:, r], ALU.add))
                dve.wait_ge(tail_summed, 1)
                do(dve.tensor_tensor(arow[0:NS, 2], arow[0:NS, 2], psum[0:NS, 4:6].rearrange("p b f -> p (b f)"), ALU.add))
                dve.wait_ge(pool_summed, TOPK)
                do(dve.memset(mv, 1.0))
                for c in range(TC):
                    t = slice(0, tok[c])
                    for h in range(2):
                        st.did(dve.bn_stats(stats[t, c, h], arow[t, c, 512 * h:512 * h + 512]))
                st.settle()
                for c in range(TC):
                    t = slice(0, tok[c])
                    st.did(dve.bn_aggr(mv[t, c, 0:2], stats[t, c]))
                st.settle()
                do(dve.tensor_scalar(mv[:, :, 1], mv[:, :, 1], EPS, None, ALU.add))
                do(dve.reciprocal(mv[:, :, 2], mv[:, :, 1]))
                dve.sem_inc(var2_ready, 1)
                dve.wait_ge(std2_ready, 1)
                do(dve.tensor_tensor(mv[:, :, 2], mv[:, :, 3], mv[:, :, 3], ALU.mult))
                do(dve.tensor_tensor(mv[:, :, 2], mv[:, :, 2], mv[:, :, 1], ALU.mult))
                do(dve.tensor_scalar(mv[:, :, 2], mv[:, :, 2], -0.5, 1.5, ALU.mult, ALU.add))
                do(dve.tensor_tensor(mv[:, :, 3], mv[:, :, 2], mv[:, :, 3], ALU.mult))
                dve.wait_ge(ln2_loaded, 16)
                for c in range(TC):
                    t = slice(0, tok[c])
                    do(dve.tensor_scalar(arow[t, c], arow[t, c], mv[t, c, 0:1], mv[t, c, 3:4], ALU.subtract, ALU.mult))
                    do(dve.tensor_tensor(arow[t, c], arow[t, c], dn[t, 1, 0], ALU.mult))
                    dve.tensor_tensor(arow[t, c], arow[t, c], dn[t, 1, 1], ALU.add).then_inc(y_ready, 1)

            @block.tensor
            def _(pe):
                def strip(slot, loads, n2, par, rhs):
                    pe.wait_ge(slot_loaded[slot], loads)
                    pe.wait_ge(bank_free[par], n2)
                    for k in range(KC):
                        ins = pe.matmul(psum[:, 5 + par, 0:T], ring[:, slot, k], rhs[:, k], start=(k == 0), stop=(k == KC - 1))
                    ins.then_inc(strips_done, 1)

                for layer, (rhs, ready) in enumerate(((ys, z_ready), (xcb, v_ready), (us, glu_ready), (ys, m_ready))):
                    pe.wait_ge(ready, 1)
                    with pe.Fori(0, 2) as g:
                        for j in range(4):
                            strip(j, g * 16 + (16 * (1 + 2 * NSEG + 2 * layer + 1)), g * 2 + (4 + 5 * NSEG + 4 * layer + j // 2), j % 2, rhs)

                def column_sums(src):
                    for k in range(KC):
                        ins = pe.matmul(psum[:, 4, 0:T], ones[:], src[:, k], start=(k == 0), stop=(k == KC - 1))
                    ins.then_inc(stat_out, 1)

                for b in range(2):
                    pe.wait_ge(bank_free[b], 4 + 5 * NSEG + 16)
                column_sums(r_)
                pe.wait_ge(stat_in, 1)
                column_sums(sq)
                pe.wait_ge(x1_ready, 1)
                pe.wait_ge(router_loaded, 16)
                for c in range(TC):
                    for k in range(KC):
                        ins = pe.matmul(psum[0:tok[c], 7, c * E:c * E + E], x1[:, k, c * P:c * P + tok[c]], wr[:, k], start=(k == 0), stop=(k == KC - 1))
                    ins.then_inc(logits_ready, 1)
                for c in range(TC):
                    if c == 2:
                        pe.wait_ge(xrow_ready, 1)
                    for k in range(KC):
                        ins = pe.transpose(psum[0:tok[c], 2 * (c % 2) + k // 4, (k % 4) * P:(k % 4) * P + P], x1[:, k, c * P:c * P + tok[c]], ident[:])
                    ins.then_inc(xrow_turned, 1)
                pe.wait_ge(xrow_ready, TC)
                pe.wait_ge(gu_in[3], 16)
                for f in range(2 * FC):
                    for k in range(KC):
                        ins = pe.matmul(psum[:, f, 0:T], gu[:, 3, k, f * P:f * P + P], x1[:, k], start=(k == 0), stop=(k == KC - 1))
                    ins.then_inc(shared_gu, 1)
                pe.wait_ge(picks_ready, 1)
                for c in range(TC + 1):
                    for b in range(min(c + 1, TC)):
                        ins = pe.matmul(psum[:, 6, c * E:c * E + E], tri[:] if b == c else ones[:], pk[:, b], start=(b == 0), stop=(b == min(c, TC - 1)))
                ins.then_inc(counted, 1)

                def select(u, pair):
                    for c in range(TC):
                        ins = pe.matmul(psum[:, 6, 0:6], S[:, u, c], val[:, c, bass.ds(pair * 2, 2)].rearrange("p e v -> p (e v)"), start=(c == 0), stop=(c == TC - 1))
                    ins.then_inc(selected, 1)

                def turn(u):
                    for k in range(KC):
                        ins = pe.transpose(psum[:, 2 + k // 4, (k % 4) * P:(k % 4) * P + P], x_rows[:, u, k * P:k * P + P], ident[:])
                    ins.then_inc(turned, 1)

                R = n_rounds(pe)
                for u in range(2):
                    pe.wait_ge(select_ready, u + 1)
                    if u:
                        pe.wait_ge(idx_ready, u)
                    select(u, u)
                pe.wait_ge(shared_h, FC)
                pe.wait_ge(dn_in[3], 16)
                for c in range(TC):
                    if c:
                        pe.wait_ge(shared_used, c)
                    for h in range(2):
                        for f in range(FC):
                            ins = pe.matmul(psum[0:tok[c], 4 + h, :], hT[:, f, c * P:c * P + tok[c]], dn[:, 3, f, h * 512:h * 512 + 512], start=(f == 0), stop=(f == FC - 1))
                    ins.then_inc(shared_dn, 1)
                pe.wait_ge(gathered[0], 16)
                turn(0)
                pe.wait_ge(shared_used, TC)
                with pe.Fori(0, R * (PAIRS // 2)) as q:
                    for u in range(2):
                        it = q * 2 + u
                        pe.wait_ge(xg_ready, it + 1)
                        for j in range(2):
                            s = 2 * u + j
                            pe.wait_ge(gu_in[s], q * 16 + (32 if s == 3 else 16))
                        for k in range(KC):
                            for j in range(2):
                                ins = pe.matmul(psum[SL * j:SL * j + SL, u, :], xg[:, u, k, SL * j:SL * j + SL], gu[:, 2 * u + j, k],
                                                start=(k == 0), stop=(k == KC - 1))
                        ins.then_inc(gu_done, 1)
                        pe.wait_ge(gathered[1 - u], q * 16 + 16 * (u + 1))
                        turn(1 - u)
                        pe.wait_ge(select_ready, it + 3)
                        pe.wait_ge(idx_ready, it + 2)
                        select(u, (it + 2) % PAIRS)
                        pe.wait_ge(hx_ready, it + 2)
                        for f in range(FC):
                            ins = pe.transpose(psum[:, 7, f * P:f * P + P], h_sl[:, f * P:f * P + P], ident[:])
                        ins.then_inc(h_turned, 1)
                        for j in range(2):
                            s = 2 * u + j
                            pe.wait_ge(dn_in[s], q * 16 + (32 if s == 3 else 16))
                        pe.wait_ge(hT_ready, it + 1)
                        pe.wait_ge(y_scaled, it + 1)
                        for h in range(2):
                            for f in range(FC):
                                for j in range(2):
                                    ins = pe.matmul(psum[SL * j:SL * j + SL, 4 + h, :], hT_sl[:, f, SL * j:SL * j + SL],
                                                    dn[:, 2 * u + j, f, h * 512:h * 512 + 512], start=(f == 0), stop=(f == FC - 1))
                        ins.then_inc(dn_done, 1)
                pe.wait_ge(y_back[2], 16)
                pe.wait_ge(eights_ready, 2)
                for h in range(2):
                    ins = pe.matmul(psum[0:NS, 4 + h, :], eights[0:NS * TOPK], dn[0:NS * TOPK, 0, 0, h * 512:h * 512 + 512], start=True, stop=True)
                ins.then_inc(tail_summed, 1)


def kernel(x_prompt, x_sample, state_conv, state_ssm_re, state_ssm_im,
           w_in, b_in, conv_w, w_conv_out, a_re, a_im, log_dt,
           ssm_b_re, ssm_b_im, ssm_c_re, ssm_c_im, ssm_d, w_glu, b_glu, w_ssm_out, w_o,
           ln1_g, ln1_b, w_router, router_bias, w_gate, w_up, w_down,
           ws_gate, ws_up, ws_down, ln2_g, ln2_b):
    import concourse.bacc as bacc
    from concourse.bass_utils import run_bass_kernel_spmd

    def a(x):
        return np.asarray(x)

    def chunks(v):
        return np.moveaxis(a(v).reshape(v.shape[:-1] + (KC, P)), -1, 0)

    def strips(w):
        return a(w).reshape(KC, P, -1, P).transpose(2, 1, 0, 3)

    def by_state(v):
        v = a(v).reshape(v.shape[:-2] + (NT, P))
        return np.moveaxis(v, -1, 0)

    f32 = np.float32
    x = np.concatenate([a(x_prompt)[0], a(x_sample)[:, 0]], axis=0)
    secs = strips(w_in[0]).reshape(6, KC, P, KC, P)
    order = [3, 1, 2, 0, 4, 5]
    w_front = np.concatenate([secs[i] for i in order] + [strips(w[0]) for w in (w_glu, w_conv_out, w_ssm_out, w_o)], axis=0)
    bin_ = chunks(a(b_in)[0].reshape(6, D)[order])
    dt = np.repeat(a(log_dt)[0][:, None], N, axis=1)
    rb = np.repeat(a(router_bias)[0][None, :], P, axis=0)
    vecs = np.concatenate([bin_.reshape(P, -1), chunks(b_glu[0]), chunks(conv_w[0]).reshape(P, -1), chunks(ssm_d[0]),
                           chunks(ln1_g[0]), chunks(ln1_b[0]), chunks(ln2_g[0]), chunks(ln2_b[0]),
                           by_state(a_re[0]), by_state(a_im[0]), by_state(dt), rb], axis=1)
    b_sm = np.zeros((P, 2, NT, 32), f32)
    c_sm = np.zeros((P, 2, NT, 32), f32)
    for r, (b, c) in enumerate(((ssm_b_re, ssm_c_re), (ssm_b_im, ssm_c_im))):
        b = a(b)[0].reshape(NT, 2, N, H)
        c = a(c)[0].reshape(NT, 2, H, N)
        for g in range(2):
            b_sm[g * N:g * N + N, r, :, g * H:g * H + H] = b[:, g].transpose(1, 0, 2)
            c_sm[g * N:g * N + N, r, :, g * H:g * H + H] = c[:, g].transpose(2, 0, 1)
    h0 = np.stack([by_state(state_ssm_re[0]), by_state(state_ssm_im[0])], axis=1).transpose(0, 1, 3, 2)
    cs = chunks(state_conv[0]).transpose(0, 3, 2, 1)

    def experts_in(g, u, n):
        w = np.concatenate([a(g).reshape(n, KC, P, F), a(u).reshape(n, KC, P, F)], axis=3)
        return w.transpose(0, 2, 1, 3).reshape(n, P, KC * 2 * F)

    def experts_out(w, n):
        return a(w).reshape(n, FC, P, D).transpose(0, 2, 1, 3).reshape(n, P, FC * D)

    arrays = {
        "x_t": x.T.reshape(KC, P, T).transpose(1, 0, 2),
        "w_front": w_front.reshape(-1, P, KC * P),
        "vecs": vecs,
        "b_sm": b_sm,
        "c_sm": c_sm,
        "h0": h0,
        "conv_state": cs,
        "w_router": a(w_router)[0].reshape(KC, P, E).transpose(1, 0, 2),
        "w_gu": np.concatenate([experts_in(w_gate[0], w_up[0], E), experts_in(ws_gate[0], ws_up[0], 1)], axis=0),
        "ln2_rows": np.stack([np.repeat(a(v)[0][None], P, axis=0) for v in (ln2_g, ln2_b)], axis=1),
        "w_dn": np.concatenate([experts_out(w_down[0], E), experts_out(ws_down[0], 1)], axis=0),
    }
    outs = {"o_y": (T, D), "o_conv_p": (P, KC, 2), "o_conv_s": (P, KC, 2, NS), "o_ssm_p": (P, 2, NT), "o_ssm_s": (P, 2, NT, NS)}
    nc = bacc.Bacc("TRN2", target_bir_lowering=False, num_devices=1)
    args = {}
    for name in arrays:
        arrays[name] = np.ascontiguousarray(arrays[name])
        args[name] = nc.dram_tensor(name, arrays[name].shape, F32, kind="ExternalInput").ap()
    for name, shape in outs.items():
        args[name] = nc.dram_tensor(name, shape, F32, kind="ExternalOutput").ap()
    build(nc, **args)
    res = run_bass_kernel_spmd(nc, [arrays], core_ids=[0]).results[0]

    y = res["o_y"]
    conv_p = res["o_conv_p"].transpose(2, 1, 0).reshape(1, 1, 2, D)
    conv_s = res["o_conv_s"].transpose(3, 2, 1, 0).reshape(1, NS, 2, D)
    ssm_p = res["o_ssm_p"].transpose(1, 2, 0).reshape(2, 1, 1, G, N)
    ssm_s = res["o_ssm_s"].transpose(1, 3, 2, 0).reshape(2, 1, NS, G, N)
    c = np.ascontiguousarray
    return (c(y[:LP].reshape(1, LP, D)), c(y[LP:].reshape(NS, 1, D)), c(conv_p), c(ssm_p[0]), c(ssm_p[1]),
            c(conv_s), c(ssm_s[0]), c(ssm_s[1]))
```

```python
from contextlib import ExitStack

import numpy as np

import concourse.bass as bass
from concourse import mybir

ALU = mybir.AluOpType
ACT = mybir.ActivationFunctionType
AX = mybir.AxisListType
F32 = mybir.dt.float32
I32 = mybir.dt.int32

P = 128
D = 1024
KC = D // P
LP = 256
NS = 8
T = LP + NS
G, H, N = 64, 16, 64
NT = G * N // P
PB = P // 32
SEG = 64
NSEG = LP // SEG
HT = NT // 2
HC = KC // 2
E = 64
F = 256
FC = F // P
TOPK, RG, TOPG = 8, 8, 4
EG = E // RG
ROUTED_SCALE = 2.5
EPS = 1e-5
ALPHA = 2.0 ** 0.25
TC = 3

US, CG, XC, BG, GA, GB = range(6)
RING = 8
PRE = KC + 4
PER_SEG = 4 * KC // NSEG
PER_HALF = PER_SEG // 2
POST = PRE + NSEG * PER_SEG
TURN_AT = KC

V_BIN = 0
V_BGLU = V_BIN + 6 * KC
V_CW = V_BGLU + KC
V_D = V_CW + 3 * KC
V_LN = V_D + KC
V_ARE = V_LN + 4 * KC
V_AIM = V_ARE + NT
V_LDT = V_AIM + NT
V_RB = V_LDT + NT
NV = V_RB + E

EXP_C = [1.0 / 5040, 1.0 / 720, 1.0 / 120, 1.0 / 24, 1.0 / 6, 0.5, 1.0, 1.0]
LN2_HI, LN2_LO = 0.693359375, -2.12194440e-4
PI2_A, PI2_B, PI2_C = 6.28125, 1.9350051879882812e-03, 3.0199159819567e-07
MAGIC = 12582912.0
GONE = -1e30


class Steps:

    def __init__(self, eng, sem):
        self.eng, self.sem, self.n = eng, sem, 0

    def did(self, ins):
        ins.then_inc(self.sem, 1)
        self.n += 1
        return self.n

    def settle(self):
        self.eng.wait_ge(self.sem, self.n)


def build(nc, x_t, w_front, vecs, b_sm, c_sm, h0, conv_state, w_router, w_gu, w_dn,
          o_y, o_conv_p, o_conv_s, o_ssm_p, o_ssm_s):
    with ExitStack() as ctx:
        def sb(name, shape, dt=F32):
            return ctx.enter_context(nc.sbuf_tensor(name, shape, dt))

        def sem(name):
            return ctx.enter_context(nc.semaphore(name))

        ring = sb("ring", [P, RING, KC, P])
        vec = sb("vec", [P, NV])
        ident = sb("ident", [P, P])
        ones = sb("ones", [P, P])
        xT = sb("xT", [P, KC, T])
        us = sb("us", [P, KC, T])
        proj = sb("proj", [P, 5 * KC, T])
        ys = sb("ys", [P, KC, T])
        cgb, xcb, bgb, gab, gbb = (proj[:, i * KC:(i + 1) * KC, :] for i in range(5))
        cst = sb("cst", [P, KC, 2, NS])
        sml = sb("sml", [P, 24, NT])

        psum = ctx.enter_context(nc.psum_tensor("banks", [P, 8, 512], F32))

        s_vec, s_x, s_bc, s_h0, s_cst = (sem(n) for n in ("vec_loaded", "x_loaded", "bc_loaded", "h0_loaded", "cst_loaded"))
        slot_loaded = [sem(f"slot{i}_loaded") for i in range(RING)]
        strips_done = sem("strips_done")
        bank_free = [sem(f"bank{i}_free") for i in range(2)]
        ident_ready = sem("ident_ready")
        before_ready = sem("before_ready")
        scores_cleared = sem("scores_cleared")
        pool_own = sem("pool_own")
        dve_own = sem("dve_own")
        dve_loop = sem("dve_loop")
        angles_ready = sem("angles_ready")
        sines_ready = sem("sines_ready")
        bb_ready = sem("bb_ready")
        bt_turned = sem("bt_turned")
        bt_ready = sem("bt_ready")
        tables_ready = sem("tables_ready")
        negc_ready = sem("negc_ready")
        seg_copied = sem("seg_copied")
        bx_ready = sem("bx_ready")
        demod_done = sem("demod_done")
        xt_ready = sem("xt_ready")
        scan_done = sem("scan_done")
        rot_done = sem("rot_done")
        h_ready = sem("h_ready")
        cy_ready = sem("cy_ready")
        y_evac = sem("y_evac")
        sx_ready = sem("sx_ready")
        sh_ready = sem("sh_ready")
        sy_ready = sem("sy_ready")
        s_fin_ready = sem("final_states_ready")
        ys_ready = sem("ys_ready")
        z_ready = sem("z_ready")
        gates_ready = sem("gates_ready")
        v_ready = sem("v_ready")
        u_ready = sem("u_ready")
        glu_ready = sem("glu_ready")
        m_ready = sem("m_ready")
        stat_in = sem("stat_in")
        stat_out = sem("stat_out")
        var_ready = sem("var_ready")
        std_ready = sem("std_ready")
        x1_ready = sem("x1_ready")
        logits_ready = sem("logits_ready")
        scores_ready = sem("scores_ready")
        router_loaded = sem("router_loaded")
        xrow_turned = sem("xrow_turned")
        xrow_ready = sem("xrow_ready")
        rows_stored = sem("rows_stored")
        picks_ready = sem("picks_ready")
        counted = sem("counted")
        lists_ready = sem("lists_ready")
        iotas_ready = sem("iotas_ready")
        gathers_cleared = sem("gathers_cleared")
        shared_gu = sem("shared_gu")
        shared_silu = sem("shared_silu")
        shared_h = sem("shared_h")
        shared_dn = sem("shared_dn")
        shared_used = sem("shared_used")
        gu_in = [sem(f"gu_slot{i}_loaded") for i in range(4)]
        dn_in = [sem(f"dn_slot{i}_loaded") for i in range(4)]
        dve_idx = sem("dve_idx")
        shifted = sem("positions_shifted")
        select_ready = sem("select_ready")
        selected = sem("selected")
        idx_ready = sem("idx_ready")
        gathered = [sem(f"gathered{i}") for i in range(2)]
        turned = sem("turned")
        xg_ready = sem("xg_ready")
        gu_done = sem("gu_done")
        silu_done = sem("silu_done")
        hx_ready = sem("hx_ready")
        dn_done = sem("dn_done")
        y_copied = sem("y_copied")
        rows_moved = sem("rows_moved")
        h_turned = sem("h_turned")
        hT_ready = sem("hT_ready")
        numbers_ready = sem("token_numbers_ready")
        sw_ready = sem("sw_ready")
        combined = sem("combined")
        added = sem("added")
        y_ready = sem("y_ready")
        stored = sem("stored")

        with ExitStack() as fctx:
            def fsb(name, shape, dt=F32):
                return fctx.enter_context(nc.sbuf_tensor(name, shape, dt))

            cosT = fsb("cosT", [P, NT, SEG])
            sinT = fsb("sinT", [P, NT, SEG])
            decay = fsb("decay", [P, NT, SEG])
            prod = fsb("prod", [P, 4, HT, SEG])
            xt = fsb("xt", [P, 2, HT, SEG])
            gg = fsb("gg", [P, 2, HT, SEG])
            hh = fsb("hh", [P, 2, 2, HT, SEG])
            bT = fsb("bT", [P, 2, KC, P])
            cS = fsb("cS", [P, 2, NT, 32])
            seg_u = fsb("seg_u", [P, KC, SEG])
            h0s = fsb("h0s", [P, 2, NT, NS])
            b_in_sm = hh[:, 0].rearrange("p r t s -> p (r t s)").rearrange("p (r t c) -> p r t c", r=2, c=32)
            bb = hh[:, 1].rearrange("p r t s -> p (r t s)").rearrange("p (r t c) -> p r t c", r=2, c=32)
            hs = hh[:, 0].rearrange("p r t s -> p r (t s)")[:, :, 0:NT * NS].rearrange("p r (t b) -> p r t b", b=NS)

            bx = psum[:, 0:4, :].rearrange("p i (c r t) -> p i c r t", c=HC, r=2)

            def bx_half(r):
                return bx[:, :, :, r, :].rearrange("p i c t -> p c i t")

            def by_ci(ap):
                return ap.rearrange("p (c i) t -> p c i t", i=PB)

            with nc.Block() as block:

                @block.sync
                def _(sp):
                    sp.dma_start(vec[:], vecs).then_inc(s_vec, 16)
                    sp.dma_start(xT[:], x_t).then_inc(s_x, 16)
                    sp.dma_start(ring[:, 0], w_front[0]).then_inc(slot_loaded[0], 16)
                    sp.dma_start(b_in_sm, b_sm).then_inc(s_bc, 16)
                    sp.dma_start(cS[:], c_sm).then_inc(s_bc, 16)
                    for n in range(1, KC):
                        sp.dma_start(ring[:, n], w_front[n]).then_inc(slot_loaded[n], 16)
                    sp.dma_start(h0s[:], h0).then_inc(s_h0, 16)
                    sp.dma_start(cst[:], conv_state).then_inc(s_cst, 16)
                    for n in range(KC, PRE):
                        sp.wait_ge(strips_done, n - 7)
                        sp.dma_start(ring[:, n % RING], w_front[n]).then_inc(slot_loaded[n % RING], 16)
                    with sp.Fori(0, NSEG) as g:
                        for s in range(PER_SEG):
                            n = g * PER_SEG + (PRE + s)
                            slot = (PRE + s) % RING
                            sp.wait_ge(strips_done, n - 7)
                            sp.dma_start(ring[:, slot], w_front[bass.ds(n, 1)].rearrange("o p f -> (o p) f")).then_inc(slot_loaded[slot], 16)
                    for n in range(POST, 6 * KC):
                        sp.wait_ge(strips_done, n - 7)
                        sp.dma_start(ring[:, n % RING], w_front[n]).then_inc(slot_loaded[n % RING], 16)
                    for j in range(4):
                        sp.wait_ge(strips_done, 5 * KC + j + 1)
                        sp.dma_start(ring[:, j], w_front[6 * KC + j]).then_inc(slot_loaded[j], 16)
                    sp.wait_ge(s_fin_ready, 1)
                    sp.dma_start(o_ssm_p, sml[:, 18:20]).then_inc(stored, 16)
                    sp.wait_ge(sh_ready, 2)
                    sp.dma_start(o_ssm_s, hs).then_inc(stored, 16)
                    sp.wait_ge(stored, 32)

                @block.gpsimd
                def _(pool):
                    pool.sem_inc(h_ready, 1)
                    st = Steps(pool, pool_own)
                    st.did(pool.memset(ones[:], 1.0))
                    st.settle()
                    pool.affine_select(out=ident[:], in_=ones[:], pattern=[[-1, P]], compare_op=ALU.is_equal,
                                       fill=0.0, base=0, channel_multiplier=1).then_inc(ident_ready, 1)
                    pool.wait_ge(s_bc, 32)
                    pool.tensor_scalar(cS[:, 1], cS[:, 1], -1.0, None, ALU.mult).then_inc(negc_ready, 1)
                    with pool.Fori(0, NSEG) as g:
                        for half in range(2):
                            k = g * 2 + half
                            pool.wait_ge(demod_done, k + 2)
                            pool.wait_ge(scan_done, k + 1)
                            pool.tensor_tensor(xt[:, 0], prod[:, 0], prod[:, 1], ALU.add).then_inc(xt_ready, 1)
                            pool.tensor_tensor(xt[:, 1], prod[:, 2], prod[:, 3], ALU.subtract).then_inc(xt_ready, 1)
                            pool.wait_ge(rot_done, k + 1)
                            pool.wait_ge(cy_ready, k + 1)
                            pool.tensor_tensor(hh[:, half, 0], prod[:, 0], prod[:, 1], ALU.subtract).then_inc(h_ready, 1)
                            pool.tensor_tensor(hh[:, half, 1], prod[:, 2], prod[:, 3], ALU.add).then_inc(h_ready, 1)

                @block.scalar
                def _(act):
                    act.sem_inc(y_evac, 1)
                    act.wait_ge(s_vec, 16)
                    for n in range(KC):
                        act.wait_ge(strips_done, n + 1)
                        act.activation(us[:, n], psum[:, 5 + n % 2, 0:T], ACT.Identity,
                                       bias=vec[:, V_BIN + n:V_BIN + n + 1]).then_inc(bank_free[n % 2], 1)
                        if n == 0:
                            act.wait_ge(angles_ready, 1)
                            act.activation(sml[:, 8:10], sml[:, 8:10], ACT.Sin).then_inc(sines_ready, 1)
                    act.wait_ge(bank_free[0], KC // 2)
                    act.wait_ge(bank_free[1], KC // 2)

                    def projected(n):
                        act.wait_ge(strips_done, n + 1)
                        act.activation(proj[:, n - KC], psum[:, 5 + n % 2, 0:T], ACT.Identity,
                                       bias=vec[:, V_BIN + n:V_BIN + n + 1]).then_inc(bank_free[n % 2], 1)

                    for n in range(KC, TURN_AT):
                        projected(n)
                    act.wait_ge(bt_turned, 1)
                    for r in range(2):
                        act.activation(bT[:, r].rearrange("p (a c) s -> p a (c s)", a=2), psum[:, 2 * r:2 * r + 2, :], ACT.Copy).then_inc(bt_ready, 1)
                    act.activation(seg_u[:], us[:, :, 0:SEG], ACT.Copy).then_inc(seg_copied, 1)
                    for n in range(TURN_AT, PRE):
                        projected(n)
                    with act.Fori(0, NSEG) as g:
                        for half in range(2):
                            for j in range(PER_HALF):
                                n = g * PER_SEG + (PRE + PER_HALF * half + j)
                                par = (PER_HALF * half + j) % 2
                                act.wait_ge(strips_done, n + 1)
                                act.activation(proj[:, bass.ds(n - KC, 1), :].rearrange("p o t -> p (o t)"), psum[:, 5 + par, 0:T], ACT.Identity,
                                               bias=vec[:, bass.ds(n + V_BIN, 1)]).then_inc(bank_free[par], 1)
                                if half == 0 and j == 1:
                                    act.wait_ge(bx_ready, g * 2 + 3)
                                    act.activation(seg_u[:], us[:, :, bass.ds(((g + 1) % NSEG) * SEG, SEG)], ACT.Copy).then_inc(seg_copied, 1)
                                if j == 2:
                                    act.wait_ge(cy_ready, g * 2 + (half + 2))
                                    at = ((g + NSEG - 1) % NSEG) * SEG if half == 0 else g * SEG
                                    act.activation(ys[:, HC * (1 - half):HC * (1 - half) + HC, bass.ds(at, SEG)],
                                                   psum[:, 4, 0:HC * SEG].rearrange("p (c t) -> p c t", c=HC), ACT.Copy).then_inc(y_evac, 1)
                    projected(POST)
                    act.wait_ge(cy_ready, 2 * NSEG + 2)
                    act.activation(ys[:, HC:KC, LP - SEG:LP], psum[:, 4, 0:HC * SEG].rearrange("p (c t) -> p c t", c=HC), ACT.Copy).then_inc(y_evac, 1)
                    for n in range(POST + 1, 6 * KC):
                        projected(n)
                    act.wait_ge(sy_ready, 1)
                    act.activation(ys[:, :, LP:T], psum[:, 4, 0:KC * NS].rearrange("p (c t) -> p c t", c=KC), ACT.Copy).then_inc(y_evac, 1)

                @block.vector
                def _(dve):
                    dve.sem_inc(scan_done, 1)
                    st = Steps(dve, dve_own)

                    def do(ins):
                        st.did(ins)
                        st.settle()

                    V = vec
                    a_re, a_im, ldt = (V[:, c:c + NT] for c in (V_ARE, V_AIM, V_LDT))
                    S = [sml[:, i] for i in range(24)]
                    dt_, ard, aid, mag, lr, li, fr, fi = S[0:8]
                    sin_, cos_, t0, t1, t2, t3 = S[8:14]

                    def exp(out, x):
                        do(dve.tensor_scalar(t0, x, 1.4426950408889634, MAGIC, ALU.mult, ALU.add))
                        do(dve.tensor_scalar(t0, t0, -MAGIC, None, ALU.add))
                        do(dve.tensor_scalar(t0, t0, -126.0, 127.0, ALU.max, ALU.min))
                        do(dve.scalar_tensor_tensor(t1, t0, -LN2_HI, x, ALU.mult, ALU.add))
                        do(dve.scalar_tensor_tensor(t1, t0, -LN2_LO, t1, ALU.mult, ALU.add))
                        do(dve.tensor_scalar(t2, t1, EXP_C[0], None, ALU.mult))
                        for c in EXP_C[1:-1]:
                            do(dve.scalar_tensor_tensor(t2, t2, c, t1, ALU.add, ALU.mult))
                        do(dve.tensor_scalar(t3.bitcast(I32), t0, 127.0, 8388608.0, ALU.add, ALU.mult))
                        do(dve.scalar_tensor_tensor(out, t2, EXP_C[-1], t3, ALU.add, ALU.mult))

                    dve.wait_ge(s_vec, 16)
                    exp(dt_, ldt)
                    do(dve.tensor_tensor(ard, a_re, dt_, ALU.mult))
                    do(dve.tensor_tensor(aid, a_im, dt_, ALU.mult))
                    do(dve.tensor_scalar(t0, aid, 0.15915494309189535, MAGIC, ALU.mult, ALU.add))
                    do(dve.tensor_scalar(t0, t0, -MAGIC, None, ALU.add))
                    do(dve.scalar_tensor_tensor(t1, t0, -PI2_A, aid, ALU.mult, ALU.add))
                    do(dve.scalar_tensor_tensor(t1, t0, -PI2_B, t1, ALU.mult, ALU.add))
                    do(dve.scalar_tensor_tensor(t1, t0, -PI2_C, t1, ALU.mult, ALU.add))
                    do(dve.tensor_scalar(sin_, t1, 3.1415925, -3.1415925, ALU.min, ALU.max))
                    do(dve.scalar_tensor_tensor(t2, sin_, -1.0, sin_, ALU.mult, ALU.max))
                    st.did(dve.tensor_scalar(cos_, t2, -1.0, 1.5707963267948966, ALU.mult, ALU.add))
                    st.settle()
                    dve.sem_inc(angles_ready, 1)
                    exp(mag, ard)
                    dve.wait_ge(sines_ready, 1)
                    do(dve.tensor_tensor(lr, mag, cos_, ALU.mult))
                    do(dve.tensor_tensor(li, mag, sin_, ALU.mult))
                    do(dve.tensor_tensor(t0, a_re, a_re, ALU.mult))
                    do(dve.tensor_tensor(t1, a_im, a_im, ALU.mult))
                    do(dve.tensor_tensor(t0, t0, t1, ALU.add))
                    do(dve.reciprocal(t0, t0))
                    do(dve.tensor_scalar(t1, lr, -1.0, None, ALU.add))
                    do(dve.tensor_tensor(t2, t1, a_re, ALU.mult))
                    do(dve.tensor_tensor(t3, li, a_im, ALU.mult))
                    do(dve.tensor_tensor(t2, t2, t3, ALU.add))
                    do(dve.tensor_tensor(fr, t2, t0, ALU.mult))
                    do(dve.tensor_tensor(t2, li, a_re, ALU.mult))
                    do(dve.tensor_tensor(t3, t1, a_im, ALU.mult))
                    do(dve.tensor_tensor(t2, t2, t3, ALU.subtract))
                    do(dve.tensor_tensor(fi, t2, t0, ALU.mult))

                    def wide(v, m):
                        return v.rearrange("p (t o) -> p t o", o=1).broadcast_to([P, NT, m])

                    dve.wait_ge(s_bc, 32)
                    tmp = prod[:, 0].rearrange("p t s -> p (t s)").rearrange("p (t c) -> p t c", c=32)
                    frw, fiw = wide(fr, 32), wide(fi, 32)
                    do(dve.tensor_tensor(tmp, b_in_sm[:, 1], fiw, ALU.mult))
                    do(dve.tensor_tensor(bb[:, 0], b_in_sm[:, 0], frw, ALU.mult))
                    do(dve.tensor_tensor(bb[:, 0], bb[:, 0], tmp, ALU.subtract))
                    do(dve.tensor_tensor(tmp, b_in_sm[:, 0], fiw, ALU.mult))
                    do(dve.tensor_tensor(bb[:, 1], b_in_sm[:, 1], frw, ALU.mult))
                    dve.tensor_tensor(bb[:, 1], bb[:, 1], tmp, ALU.add).then_inc(bb_ready, 1)

                    do(dve.memset(cosT[:, :, 0:1], 1.0))
                    do(dve.memset(sinT[:, :, 0:1], 0.0))
                    vc, vs, wc, ws = cos_, sin_, S[14], S[15]
                    m = 1
                    while m < SEG:
                        c0, s0 = cosT[:, :, 0:m], sinT[:, :, 0:m]
                        c1, s1 = cosT[:, :, m:2 * m], sinT[:, :, m:2 * m]
                        pa = prod[:, 0:2].rearrange("p a t s -> p (a t) s")[:, :, 0:m]
                        pb = prod[:, 2:4].rearrange("p a t s -> p (a t) s")[:, :, 0:m]
                        st.did(dve.tensor_tensor(c1, c0, wide(vc, m), ALU.mult))
                        st.did(dve.tensor_tensor(pa, s0, wide(vs, m), ALU.mult))
                        st.did(dve.tensor_tensor(s1, s0, wide(vc, m), ALU.mult))
                        do(dve.tensor_tensor(pb, c0, wide(vs, m), ALU.mult))
                        st.did(dve.tensor_tensor(c1, c1, pa, ALU.subtract))
                        st.did(dve.tensor_tensor(s1, s1, pb, ALU.add))
                        st.did(dve.tensor_tensor(t0, vc, vc, ALU.mult))
                        st.did(dve.tensor_tensor(t1, vs, vs, ALU.mult))
                        do(dve.tensor_tensor(t2, vc, vs, ALU.mult))
                        st.did(dve.tensor_tensor(wc, t0, t1, ALU.subtract))
                        do(dve.tensor_scalar(ws, t2, 2.0, None, ALU.mult))
                        vc, vs, wc, ws = wc, ws, (S[16] if wc is S[14] else S[14]), (S[17] if ws is S[15] else S[15])
                        m *= 2
                    do(dve.tensor_copy(decay[:], wide(mag, SEG)))
                    dve.memset(decay[:, :, 0:1], 0.0).then_inc(tables_ready, 1)
                    dve.wait_ge(tables_ready, 1)

                    dve.wait_ge(bt_turned, 1)
                    for half in range(2):
                        do(dve.memset(hh[:, half, :, :, SEG - 1:SEG], 0.0))
                    dve.sem_inc(demod_done, 1)
                    with dve.Fori(0, NSEG) as g:
                        for half in range(2):
                            k = g * 2 + half
                            tiles = slice(HT * half, HT * half + HT)
                            ct, sn = by_ci(cosT[:, tiles]), by_ci(sinT[:, tiles])
                            dve.wait_ge(bx_ready, k + 2)
                            dve.wait_ge(h_ready, k * 2 + 1)
                            dve.tensor_tensor(by_ci(prod[:, 0]), bx_half(0), ct, ALU.mult)
                            dve.tensor_tensor(by_ci(prod[:, 1]), bx_half(1), sn, ALU.mult)
                            dve.tensor_tensor(by_ci(prod[:, 2]), bx_half(1), ct, ALU.mult)
                            dve.tensor_tensor(by_ci(prod[:, 3]), bx_half(0), sn, ALU.mult).then_inc(demod_done, 1)
                            base = g * (2 * 6) + 6 * half
                            c = sml[:, 18:22, 0:HT]
                            hr, hi = hh[:, half, 0, :, SEG - 1], hh[:, half, 1, :, SEG - 1]
                            lrh, lih = lr[:, tiles], li[:, tiles]
                            first = [xt[:, 0, :, 0], xt[:, 1, :, 0]]
                            dve.tensor_tensor(c[:, 0], lrh, hr, ALU.mult).then_inc(dve_loop, 1)
                            dve.tensor_tensor(c[:, 1], lih, hi, ALU.mult).then_inc(dve_loop, 1)
                            dve.tensor_tensor(c[:, 2], lrh, hi, ALU.mult).then_inc(dve_loop, 1)
                            dve.tensor_tensor(c[:, 3], lih, hr, ALU.mult).then_inc(dve_loop, 1)
                            dve.wait_ge(dve_loop, base + 4)
                            dve.tensor_tensor(c[:, 0], c[:, 0], c[:, 1], ALU.subtract).then_inc(dve_loop, 1)
                            dve.tensor_tensor(c[:, 2], c[:, 2], c[:, 3], ALU.add).then_inc(dve_loop, 1)
                            dve.wait_ge(dve_loop, base + 6)
                            dve.wait_ge(xt_ready, k * 2 + 2)
                            dve.tensor_tensor(first[0], first[0], c[:, 0], ALU.add).then_inc(sx_ready, 1)
                            dve.tensor_tensor(first[1], first[1], c[:, 2], ALU.add).then_inc(sx_ready, 1)
                            dve.wait_ge(sx_ready, k * 2 + 2)
                            dec = decay[:, tiles].rearrange("p t s -> p (t s)")
                            for r in range(2):
                                ins = dve.tensor_tensor_scan(gg[:, r].rearrange("p t s -> p (t s)"), dec,
                                                             xt[:, r].rearrange("p t s -> p (t s)"), 0.0, ALU.mult, ALU.add)
                            ins.then_inc(scan_done, 1)
                            dve.wait_ge(scan_done, k + 2)
                            ct, sn = cosT[:, tiles], sinT[:, tiles]
                            dve.tensor_tensor(prod[:, 0], gg[:, 0], ct, ALU.mult)
                            dve.tensor_tensor(prod[:, 1], gg[:, 1], sn, ALU.mult)
                            dve.tensor_tensor(prod[:, 2], gg[:, 1], ct, ALU.mult)
                            dve.tensor_tensor(prod[:, 3], gg[:, 0], sn, ALU.mult).then_inc(rot_done, 1)
                    fin = sml[:, 18:20]
                    dve.wait_ge(h_ready, 4 * NSEG + 1)
                    for r in range(2):
                        for half in range(2):
                            do(dve.tensor_copy(fin[:, r, half * HT:half * HT + HT], hh[:, half, r, :, SEG - 1]))
                    dve.sem_inc(s_fin_ready, 1)
                    dve.wait_ge(s_h0, 16)
                    dve.wait_ge(cy_ready, 2 * NSEG + 2)
                    q = [prod[:, i].rearrange("p t s -> p (t s)")[:, 0:NT * NS].rearrange("p (t b) -> p t b", b=NS) for i in range(4)]
                    do(dve.tensor_tensor(q[0], h0s[:, 0], wide(lr, NS), ALU.mult))
                    do(dve.tensor_tensor(q[1], h0s[:, 1], wide(li, NS), ALU.mult))
                    do(dve.tensor_tensor(q[2], h0s[:, 1], wide(lr, NS), ALU.mult))
                    do(dve.tensor_tensor(q[3], h0s[:, 0], wide(li, NS), ALU.mult))
                    do(dve.tensor_tensor(q[0], q[0], q[1], ALU.subtract))
                    do(dve.tensor_tensor(q[2], q[2], q[3], ALU.add))
                    for b in range(2):
                        dve.wait_ge(bank_free[b], 2 * KC)
                    dve.wait_ge(s_cst, 16)
                    do(dve.tensor_tensor(cgb, cgb, xcb, ALU.mult))
                    dve.sem_inc(u_ready, 1)

                    def cw(k, n):
                        return V[:, V_CW + k * KC + n:V_CW + k * KC + n + 1]

                    for n in range(KC):
                        st.did(dve.tensor_scalar(xcb[:, n], cgb[:, n], cw(2, n), None, ALU.mult))
                    st.settle()
                    for n in range(KC):
                        st.did(dve.scalar_tensor_tensor(xcb[:, n, 1:LP], cgb[:, n, 0:LP - 1], cw(1, n), xcb[:, n, 1:LP], ALU.mult, ALU.add))
                        st.did(dve.scalar_tensor_tensor(xcb[:, n, LP:T], cst[:, n, 1], cw(1, n), xcb[:, n, LP:T], ALU.mult, ALU.add))
                    st.settle()
                    for n in range(KC):
                        st.did(dve.scalar_tensor_tensor(xcb[:, n, 2:LP], cgb[:, n, 0:LP - 2], cw(0, n), xcb[:, n, 2:LP], ALU.mult, ALU.add))
                        st.did(dve.scalar_tensor_tensor(xcb[:, n, LP:T], cst[:, n, 0], cw(0, n), xcb[:, n, LP:T], ALU.mult, ALU.add))
                    st.settle()
                    do(dve.tensor_tensor(xcb, xcb, bgb, ALU.mult))
                    dve.sem_inc(v_ready, 1)
                    dve.wait_ge(bx_ready, 2 * NSEG + 3)
                    sx = psum[:, 0:4, 0:2 * KC * NS].rearrange("p i (c r b) -> p i c r b", c=KC, r=2)
                    for r in range(2):
                        dve.tensor_tensor(by_ci(hs[:, r]), sx[:, :, :, r, :].rearrange("p i c b -> p c i b"),
                                          by_ci(q[2 * r]), ALU.add).then_inc(sh_ready, 1)

                @block.tensor
                def _(pe):
                    def state_input(half, n):
                        c, i, r = n // (2 * PB), n // 2 % PB, n % 2
                        rows = slice(32 * i, 32 * i + 32)
                        ins = pe.matmul(bx[:, i, c, r, :], bT[rows, r, HC * half + c, :], seg_u[rows, HC * half + c, :], start=True, stop=True)
                        if n == 2 * HT - 1:
                            ins.then_inc(bx_ready, 1)

                    def output(half, t, r):
                        c, i = t // PB, t % PB
                        ins = pe.matmul(psum[32 * i:32 * i + 32, 4, SEG * c:SEG * c + SEG], cS[:, r, HT * half + t],
                                        hh[:, half, r, t], start=(r == 0), stop=(r == 1))
                        if (t, r) == (HT - 1, 1):
                            ins.then_inc(cy_ready, 1)

                    pe.sem_inc(cy_ready, 1)
                    pe.sem_inc(bx_ready, 1)
                    pe.wait_ge(s_x, 16)
                    for n in range(PRE):
                        if n == TURN_AT:
                            pe.wait_ge(ident_ready, 1)
                            pe.wait_ge(bb_ready, 1)
                            for r in range(2):
                                for c in range(KC):
                                    ins = pe.transpose(psum[:, 2 * r + c // 4, (c % 4) * P:(c % 4) * P + P],
                                                       bb[:, r, PB * c:PB * c + PB].rearrange("p t c -> p (t c)"), ident[:])
                            ins.then_inc(bt_turned, 1)
                        if n == TURN_AT + 1:
                            pe.wait_ge(bt_ready, 2)
                            pe.wait_ge(negc_ready, 1)
                            pe.wait_ge(seg_copied, 1)
                        pe.wait_ge(slot_loaded[n % RING], 16 + 16 * (n // RING))
                        if n >= 2:
                            pe.wait_ge(bank_free[n % 2], n // 2)
                        for k in range(KC):
                            ins = pe.matmul(psum[:, 5 + n % 2, 0:T], ring[:, n % KC, k], xT[:, k], start=(k == 0), stop=(k == KC - 1))
                            if k == KC - 1:
                                ins.then_inc(strips_done, 1)
                            if n == TURN_AT + 1:
                                for m in range(4):
                                    state_input(0, 4 * k + m)
                    with pe.Fori(0, NSEG) as g:
                        for half in range(2):
                            k = g * 2 + half
                            for j in range(PER_HALF):
                                if j == 0:
                                    pe.wait_ge(demod_done, k + 2)
                                    if half == 1:
                                        pe.wait_ge(seg_copied, g + 2)
                                if j == 2:
                                    pe.wait_ge(h_ready, k * 2 + 1)
                                    pe.wait_ge(y_evac, k + 1)
                                s = PER_HALF * half + j
                                slot = (PRE + s) % RING
                                pe.wait_ge(slot_loaded[slot], g * 16 + (16 + 16 * ((PRE + s) // RING)))
                                pe.wait_ge(bank_free[s % 2], g * PER_HALF + (PRE + s) // 2)
                                for kc in range(KC):
                                    ins = pe.matmul(psum[:, 5 + s % 2, 0:T], ring[:, slot, kc], xT[:, kc], start=(kc == 0), stop=(kc == KC - 1))
                                    if kc == KC - 1:
                                        ins.then_inc(strips_done, 1)
                                    if j < 2:
                                        for r in range(2):
                                            state_input(1 - half, (j * KC + kc) * 2 + r)
                                    elif j == 2:
                                        for n in range(4):
                                            output(1 - half, 2 * kc + n // 2, n % 2)
                    sx = psum[:, 0:4, 0:2 * KC * NS].rearrange("p i (c r b) -> p i c r b", c=KC, r=2)
                    for n in range(POST, 6 * KC):
                        if n == POST:
                            pe.wait_ge(h_ready, 4 * NSEG + 1)
                            pe.wait_ge(y_evac, 2 * NSEG + 1)
                        elif n == POST + 1:
                            pe.wait_ge(demod_done, 2 * NSEG + 1)
                        elif n == POST + 3:
                            pe.wait_ge(sh_ready, 2)
                            pe.wait_ge(y_evac, 2 * NSEG + 2)
                        pe.wait_ge(slot_loaded[n % RING], 16 + 16 * (n // RING))
                        pe.wait_ge(bank_free[n % 2], n // 2)
                        for kc in range(KC):
                            ins = pe.matmul(psum[:, 5 + n % 2, 0:T], ring[:, n % RING, kc], xT[:, kc], start=(kc == 0), stop=(kc == KC - 1))
                            if kc == KC - 1:
                                ins.then_inc(strips_done, 1)
                            if n == POST:
                                for m in range(4):
                                    output(1, 2 * kc + m // 2, m % 2)
                            elif n < POST + 3:
                                for m in range(4):
                                    at = ((n - POST - 1) * KC + kc) * 4 + m
                                    c, i, r = at // (2 * PB), at // 2 % PB, at % 2
                                    rows = slice(32 * i, 32 * i + 32)
                                    ins = pe.matmul(sx[:, i, c, r, :], bT[rows, r, c, :], us[rows, c, LP:T], start=True, stop=True)
                                if at == 2 * NT - 1:
                                    ins.then_inc(bx_ready, 1)
                            else:
                                for i in range(PB):
                                    for r in range(2):
                                        ins = pe.matmul(psum[32 * i:32 * i + 32, 4, NS * kc:NS * kc + NS], cS[:, r, PB * kc + i], hs[:, r, PB * kc + i],
                                                        start=(r == 0), stop=(r == 1))
                                if kc == KC - 1:
                                    ins.then_inc(sy_ready, 1)
        SL = 64
        SLOTS = 4
        PAIRS = E // 2
        BIG = float(1 << 20)
        gu = sb("gu", [P, SLOTS, KC, 2 * F])
        dn = sb("dn", [P, SLOTS, FC, D])
        wr = sb("wr", [P, KC, E])
        tri = sb("tri", [P, P])

        def carve(t, pattern, *shapes):
            flat, at, out = t.rearrange(pattern), 0, []
            for shape in shapes:
                n = int(np.prod(shape))
                names = "abcd"[:len(shape)]
                v = flat[:, at:at + n].rearrange(f"p ({' '.join(names)}) -> p {' '.join(names)}", **{m: k for m, k in zip(names, shape)})
                out.append(v)
                at += n
            assert at <= flat.shape[1], (at, flat.shape)
            return out

        x_rows, xg, y_rows, hT, sil, hT_sl, h_sl, sil_sl = carve(
            ring[:], "p s k m -> p (s k m)", (2, D), (2, KC, P), (2, D), (FC, T), (FC, T), (FC, 2 * SL), (F,), (F,))
        xrow, = carve(proj[:, 2 * KC:5 * KC], "p s t -> p (s t)", (TC, D))
        scores, rt, top8, cmp, before = carve(ys[:], "p k t -> p (k t)", (TC, E), (5, TC, E), (TC, RG, 8), (TC, RG, RG), (RG, RG))
        val, pos, S, iota, pk, small = carve(xT[:], "p k t -> p (k t)", (TC, E, 2), (TC, E), (2, TC, 2 * SL), (SL,), (TC, E), (64,))
        token_no, sw = carve(us[:], "p k t -> p (k t)", (T,), (2, T))
        meta, dest = carve(sml[:], "p a t -> p (a t)", (2, 2), (2, 1))
        rounds = sb("rounds", [P, 1], I32)
        idx = sb("idx", [P, 2], mybir.dt.uint32)
        r_, x1, sq = xcb, cgb, us
        acc = xcb
        mu = sb("mu", [P, 3, T])
        tok = [P, P, NS]
        x_dram = nc.dram_tensor("x_rows_dram", [T, D], F32, kind="Internal").ap()
        tokid = small[:, 0:TC]

        with nc.Block() as block:

            def n_rounds(eng):
                eng.wait_ge(lists_ready, 1)
                return eng.value_load(rounds[0:1, 0:1], min_val=1, max_val=5)

            @block.sync
            def _(sp):
                sp.dma_start(wr[:], w_router).then_inc(router_loaded, 16)
                parts = [("gu", E, 3), ("dn", E, 3), ("gu", 0, 0), ("gu", 1, 1), ("dn", 0, 0), ("dn", 1, 1), ("gu", 2, 2)]
                for g in range(1, 8):
                    for j in range(4):
                        n = 6 * KC + 4 * g + j
                        sp.wait_ge(strips_done, n - 3)
                        sp.dma_start(ring[:, j], w_front[n]).then_inc(slot_loaded[j], 16)
                    kind, e, s = parts[g - 1]
                    if kind == "gu":
                        sp.dma_start(gu[:, s], w_gu[e]).then_inc(gu_in[s], 16)
                    else:
                        sp.dma_start(dn[:, s], w_dn[e]).then_inc(dn_in[s], 16)
                sp.dma_start(dn[:, 2], w_dn[2]).then_inc(dn_in[2], 16)
                sp.wait_ge(u_ready, 1)
                sp.dma_start(o_conv_p, cgb[:, :, LP - 2:LP]).then_inc(stored, 16)
                sp.dma_start(o_conv_s[:, :, 0], cst[:, :, 1]).then_inc(stored, 16)
                sp.dma_start(o_conv_s[:, :, 1], cgb[:, :, LP:T]).then_inc(stored, 16)
                for c in range(TC):
                    sp.wait_ge(xrow_ready, c + 1)
                    sp.dma_start(x_dram[c * P:c * P + tok[c]], xrow[0:tok[c], c]).then_inc(rows_stored, 16)
                sp.wait_ge(shared_gu, 2 * FC)
                sp.dma_start(gu[:, 3], w_gu[3]).then_inc(gu_in[3], 16)
                sp.wait_ge(shared_dn, KC)
                sp.dma_start(dn[:, 3], w_dn[3]).then_inc(dn_in[3], 16)
                R = n_rounds(sp)
                all_gathered = sp.snap(R * (16 * PAIRS // 2) + 16)
                with sp.Fori(1, R * (PAIRS // 2)) as q:
                    for s in range(SLOTS):
                        e = (q * SLOTS + s) % E
                        sp.wait_ge(gu_done, q * 2 + (s // 2 - 1))
                        sp.dma_start(gu[:, s], w_gu[bass.ds(e, 1)].rearrange("o p f -> (o p) f")).then_inc(gu_in[s], 16)
                        sp.wait_ge(dn_done, q * 2 + (s // 2 - 1))
                        sp.dma_start(dn[:, s], w_dn[bass.ds(e, 1)].rearrange("o p f -> (o p) f")).then_inc(dn_in[s], 16)
                for u in range(2):
                    sp.wait_ge(gathered[u], all_gathered)
                for h in range(2):
                    sp.wait_ge(y_ready, HC * (h + 1))
                    sp.dma_start(o_y[:, HC * h:HC * h + HC], x1[:, HC * h:HC * h + HC]).then_inc(stored, 16)
                sp.wait_ge(stored, 16 * 7)

            @block.gpsimd
            def _(pool):
                pool.affine_select(out=tri[:], in_=ones[:], pattern=[[1, P]], compare_op=ALU.is_gt,
                                   fill=0.0, base=0, channel_multiplier=-1).then_inc(before_ready, 1)
                pool.wait_ge(strips_done, 10 * KC)
                pool.affine_select(out=before, in_=ones[:, 0:RG * RG].rearrange("p (g h) -> p g h", g=RG), pattern=[[1, RG], [-1, RG]],
                                   compare_op=ALU.is_gt, fill=0.0, base=0, channel_multiplier=0).then_inc(before_ready, 1)
                pool.memset(x_rows, 0.0).then_inc(gathers_cleared, 1)
                for b in range(2):
                    pool.wait_ge(bank_free[b], 3 * KC + 16)
                pool.iota(iota, pattern=[[1, SL]], base=0, channel_multiplier=0, allow_small_or_imprecise_dtypes=True).then_inc(iotas_ready, 1)
                pool.iota(tokid, pattern=[[P, TC]], base=1, channel_multiplier=1, allow_small_or_imprecise_dtypes=True).then_inc(iotas_ready, 1)
                pool.wait_ge(stat_out, 2)
                pool.iota(token_no, pattern=[[1, T]], base=1, channel_multiplier=0, allow_small_or_imprecise_dtypes=True).then_inc(numbers_ready, 1)
                pool.wait_ge(rows_stored, 16 * TC)
                pool.wait_ge(gathers_cleared, 1)
                R = n_rounds(pool)

                last_x = pool.to_reg(T - 1)

                def gather(u):
                    pool.sem_inc(rows_moved, 1)
                    pool.indirect_dma_start(x_rows[:, u], None, x_dram, bass.IndirectOffsetOnAxis(ap=idx[:, u:u + 1], axis=0),
                                            bounds_check=last_x, oob_is_err=False).then_inc(gathered[u], 16)

                for u in range(2):
                    pool.wait_ge(idx_ready, u + 1)
                    gather(u)
                with pool.Fori(0, R * (PAIRS // 2)) as q:
                    for u in range(2):
                        it = q * 2 + u
                        pool.wait_ge(idx_ready, it + 3)
                        pool.wait_ge(turned, it + 1)
                        gather(u)

            @block.scalar
            def _(act):
                act.sem_inc(y_copied, 1)
                act.wait_ge(bank_free[0], 3 * KC)
                act.wait_ge(bank_free[1], 3 * KC)
                act.activation(proj[:, 3 * KC:5 * KC], proj[:, 3 * KC:5 * KC], ACT.Sigmoid).then_inc(gates_ready, 1)
                act.wait_ge(ys_ready, 1)
                act.activation(ys[:], ys[:], ACT.Gelu_apprx_tanh).then_inc(z_ready, 1)
                for n in range(KC):
                    act.wait_ge(strips_done, 7 * KC + n + 1)
                    act.activation(us[:, n], psum[:, 5 + n % 2, 0:T], ACT.Sigmoid,
                                   bias=vec[:, V_BGLU + n:V_BGLU + n + 1]).then_inc(bank_free[n % 2], 1)

                act.wait_ge(var_ready, 1)
                act.activation(mu[:, 1], mu[:, 1], ACT.Sqrt).then_inc(std_ready, 1)
                act.wait_ge(scores_cleared, 1)
                act.wait_ge(logits_ready, TC)
                for c in range(TC):
                    act.activation(scores[0:tok[c], c], psum[0:tok[c], 7, c * E:c * E + E], ACT.Sigmoid).then_inc(scores_ready, 1)
                for c in range(TC):
                    act.wait_ge(xrow_turned, c + 1)
                    act.activation(xrow[0:tok[c], c], psum[0:tok[c], 2 * (c % 2):2 * (c % 2) + 2].rearrange("p b f -> p (b f)"), ACT.Copy).then_inc(xrow_ready, 1)
                act.wait_ge(shared_gu, 2 * FC)
                for f in range(FC):
                    act.activation(sil[:, f], psum[:, f, 0:T], ACT.Silu).then_inc(shared_silu, 1)
                R = n_rounds(act)

                def rows_in(u, it):
                    act.wait_ge(turned, it)
                    act.activation(xg[:, u].rearrange("p (b k) s -> p b (k s)", b=2), psum[:, 2:4], ACT.Copy).then_inc(xg_ready, 1)

                rows_in(0, 1)
                with act.Fori(0, R * (PAIRS // 2)) as q:
                    for u in range(2):
                        it = q * 2 + u
                        act.wait_ge(gu_done, it + 1)
                        act.wait_ge(hx_ready, it + 1)
                        act.activation(sil_sl, psum[:, u, 0:F], ACT.Silu).then_inc(silu_done, 1)
                        rows_in(1 - u, it + 2)
                        act.wait_ge(h_turned, it + 1)
                        act.activation(hT_sl.rearrange("p f s -> p (f s)"), psum[:, 7, 0:FC * 2 * SL], ACT.Copy).then_inc(hT_ready, 1)
                        act.wait_ge(dn_done, it + 1)
                        act.wait_ge(combined, it * KC + 1)
                        act.activation(y_rows[:, u], psum[:, 4:6].rearrange("p b f -> p (b f)"), ACT.Copy).then_inc(y_copied, 1)
                act.wait_ge(var_ready, 2)
                act.activation(mu[:, 1], mu[:, 1], ACT.Sqrt).then_inc(std_ready, 1)

            @block.vector
            def _(dve):
                st = Steps(dve, dve_loop)
                st.n = 12 * NSEG
                V = vec
                dve.sem_inc(hx_ready, 1)

                def do(ins):
                    st.did(ins)
                    st.settle()

                dve.wait_ge(y_evac, 2 * NSEG + 3)
                for n in range(KC):
                    st.did(dve.scalar_tensor_tensor(ys[:, n], us[:, n], V[:, V_D + n:V_D + n + 1], ys[:, n], ALU.mult, ALU.add))
                st.settle()
                dve.sem_inc(ys_ready, 1)
                dve.wait_ge(gates_ready, 1)
                for n in range(KC):
                    dve.wait_ge(strips_done, 6 * KC + n + 1)
                    dve.tensor_tensor(bgb[:, n], psum[:, 5 + n % 2, 0:T], gab[:, n], ALU.mult).then_inc(bank_free[n % 2], 1)
                for n in range(KC):
                    dve.wait_ge(bank_free[n % 2], 3 * KC + 4 + n // 2 + 1)
                    st.did(dve.tensor_tensor(us[:, n], ys[:, n], us[:, n], ALU.mult))
                st.settle()
                dve.sem_inc(glu_ready, 1)
                for n in range(KC):
                    dve.wait_ge(strips_done, 8 * KC + n + 1)
                    dve.tensor_tensor(gbb[:, n], psum[:, 5 + n % 2, 0:T], gbb[:, n], ALU.mult).then_inc(bank_free[n % 2], 1)
                    dve.wait_ge(bank_free[n % 2], 3 * KC + 4 + 4 + n // 2 + 1)
                    do(dve.tensor_tensor(ys[:, n], gbb[:, n], bgb[:, n], ALU.add))
                dve.sem_inc(m_ready, 1)
                for n in range(KC):
                    dve.wait_ge(strips_done, 9 * KC + n + 1)
                    dve.scalar_tensor_tensor(xcb[:, n], xT[:, n], ALPHA, psum[:, 5 + n % 2, 0:T], ALU.mult, ALU.add).then_inc(bank_free[n % 2], 1)

                def norm(nth, src):
                    wide = mu[:, 0:1].broadcast_to([P, KC, T])
                    dve.wait_ge(stat_out, 2 * nth + 1)
                    do(dve.tensor_scalar(mu[:, 0], psum[:, 4, 0:T], 1.0 / D, None, ALU.mult))
                    do(dve.tensor_tensor(src, src, wide, ALU.subtract))
                    do(dve.tensor_tensor(sq[:], src, src, ALU.mult))
                    dve.sem_inc(stat_in, 1)
                    dve.wait_ge(stat_out, 2 * nth + 2)
                    do(dve.tensor_scalar(mu[:, 0], psum[:, 4, 0:T], 1.0 / D, EPS, ALU.mult, ALU.add))
                    do(dve.reciprocal(mu[:, 1], mu[:, 0]))
                    dve.sem_inc(var_ready, 1)
                    dve.wait_ge(std_ready, nth + 1)
                    do(dve.tensor_tensor(mu[:, 2], mu[:, 1], mu[:, 1], ALU.mult))
                    do(dve.tensor_tensor(mu[:, 2], mu[:, 2], mu[:, 0], ALU.mult))
                    do(dve.tensor_scalar(mu[:, 2], mu[:, 2], -0.5, 1.5, ALU.mult, ALU.add))
                    do(dve.tensor_tensor(mu[:, 0], mu[:, 2], mu[:, 1], ALU.mult))
                    do(dve.tensor_tensor(src, src, wide, ALU.mult))

                norm(0, r_)
                dve.wait_ge(stored, 16 * 5)
                for n in range(KC):
                    st.did(dve.tensor_scalar(x1[:, n], r_[:, n], vec[:, V_LN + n:V_LN + n + 1], vec[:, V_LN + KC + n:V_LN + KC + n + 1], ALU.mult, ALU.add))
                st.settle()
                dve.sem_inc(x1_ready, 1)

                biased, masked, left, picked, wts = (rt[:, i] for i in range(5))
                gs, rank, cnt = (small[:, 6 + 8 * i:6 + 8 * i + 8] for i in range(3))
                total, cm, over = small[:, 30:33], small[:, 33:34], small[:, 34:38]
                dve.memset(scores, 0.5).then_inc(scores_cleared, 1)
                dve.wait_ge(iotas_ready, 2)
                do(dve.memset(pk, 0.0))
                dve.wait_ge(scores_ready, TC)
                rb = vec[:, V_RB:V_RB + E].rearrange("p (o e) -> p o e", o=1).broadcast_to([P, TC, E])
                do(dve.tensor_tensor(biased, scores, rb, ALU.add))
                for c in range(TC):
                    for g in range(RG):
                        st.did(dve.max(top8[:, c, g], biased[:, c, g * EG:g * EG + EG]))
                st.settle()
                dve.wait_ge(before_ready, 2)
                for c in range(TC):
                    do(dve.tensor_tensor(gs, top8[:, c, :, 0], top8[:, c, :, 1], ALU.add))
                    me = gs.rearrange("p (g o) -> p g o", o=1).broadcast_to([P, RG, RG])
                    other = gs.rearrange("p (o g) -> p o g", o=1).broadcast_to([P, RG, RG])
                    eq = cmp[:, c]
                    do(dve.tensor_tensor(eq, other, me, ALU.is_equal))
                    do(dve.tensor_tensor(eq, eq, before, ALU.mult))
                    do(dve.tensor_reduce(cnt, eq, AX.X, ALU.add))
                    do(dve.tensor_tensor(eq, other, me, ALU.is_gt))
                    do(dve.tensor_reduce(rank, eq, AX.X, ALU.add))
                    do(dve.tensor_tensor(rank, rank, cnt, ALU.add))
                    do(dve.tensor_scalar(rank, rank, float(TOPG), None, ALU.is_lt))
                    do(dve.tensor_scalar(rank, rank, -GONE, GONE, ALU.mult, ALU.add))
                    gm = rank.rearrange("p (g o) -> p g o", o=1).broadcast_to([P, RG, EG])
                    do(dve.tensor_tensor(masked[:, c].rearrange("p (g e) -> p g e", g=RG), biased[:, c].rearrange("p (g e) -> p g e", g=RG), gm, ALU.add))
                    do(dve.max(top8[:, c, 0], masked[:, c]))
                    do(dve.match_replace(left[:, c], top8[:, c, 0], masked[:, c], 3 * GONE))
                do(dve.tensor_tensor(picked, left, masked, ALU.not_equal))
                st.did(dve.tensor_copy(pk[:, 0:2], picked[:, 0:2]))
                st.did(dve.tensor_copy(pk[0:NS, 2], picked[0:NS, 2]))
                st.settle()
                dve.sem_inc(picks_ready, 1)
                do(dve.tensor_tensor(wts, scores, picked, ALU.mult))
                do(dve.tensor_reduce(total, wts, AX.X, ALU.add))
                do(dve.reciprocal(total, total))
                for c in range(TC):
                    st.did(dve.tensor_scalar(val[:, c, :, 0], wts[:, c], total[:, c:c + 1], ROUTED_SCALE, ALU.mult, ALU.mult))
                    st.did(dve.tensor_scalar(val[:, c, :, 1], pk[:, c], 0.0, tokid[:, c:c + 1], ALU.mult, ALU.add))
                st.settle()
                do(dve.tensor_scalar(left, pk, -1000.0, 1000.0, ALU.mult, ALU.add))
                dve.wait_ge(counted, 1)
                st.did(dve.tensor_tensor(pos, psum[:, 6, 0:TC * E].rearrange("p (c e) -> p c e", c=TC), left, ALU.add))
                do(dve.tensor_reduce(cm, psum[:, 6, TC * E:TC * E + E], AX.X, ALU.max))
                for i in range(4):
                    st.did(dve.tensor_scalar(over[:, i:i + 1], cm, float(SL * (i + 1)), None, ALU.is_gt))
                st.settle()
                do(dve.tensor_reduce(cm, over, AX.X, ALU.add))
                do(dve.tensor_scalar(rounds[:], cm, 1.0, None, ALU.add))
                dve.sem_inc(lists_ready, 1)
                R = n_rounds(dve)

                def select(u, pair, nth):
                    p2 = pos[:, :, bass.ds(pair * 2, 2)]
                    dve.tensor_tensor(S[:, u].rearrange("p c (j s) -> p c j s", j=2),
                                      iota.rearrange("p (c j s) -> p c j s", c=1, j=1).broadcast_to([P, TC, 2, SL]),
                                      p2.rearrange("p c (j s) -> p c j s", s=1).broadcast_to([P, TC, 2, SL]), ALU.is_equal).then_inc(select_ready, 1)
                    dve.wait_ge(select_ready, nth)
                    dve.tensor_scalar(p2, p2, -float(SL), None, ALU.add).then_inc(shifted, 1)

                def indices(u, base):
                    for j in range(2):
                        h = slice(SL * j, SL * j + SL)
                        dve.tensor_copy(meta[h, u], psum[h, 6, 2 * j:2 * j + 2]).then_inc(dve_idx, 1)
                    dve.wait_ge(dve_idx, base + 2)
                    dve.tensor_scalar(dest[:, u], meta[:, u, 1:2], 0.0, BIG, ALU.is_equal, ALU.mult).then_inc(dve_idx, 1)
                    dve.wait_ge(dve_idx, base + 3)
                    dve.scalar_tensor_tensor(idx[:, u:u + 1], meta[:, u, 1:2], -1.0, dest[:, u], ALU.add, ALU.add).then_inc(idx_ready, 1)

                for u in range(2):
                    select(u, u, u + 1)
                    dve.wait_ge(selected, u + 1)
                    indices(u, 3 * u)
                for f in range(FC):
                    dve.wait_ge(shared_silu, f + 1)
                    dve.tensor_tensor(hT[:, f], sil[:, f], psum[:, FC + f, 0:T], ALU.mult).then_inc(shared_h, 1)
                for n in range(KC):
                    dve.wait_ge(shared_dn, n + 1)
                    dve.scalar_tensor_tensor(acc[:, n], x1[:, n], ALPHA, psum[:, 4 + n % 2, 0:T], ALU.mult, ALU.add).then_inc(shared_used, 1)
                dve.wait_ge(numbers_ready, 1)
                st.did(dve.memset(sw[:, 1], 0.0))
                st.did(dve.memset(y_rows[:, 1], 0.0))
                st.settle()
                dve.wait_ge(shared_used, KC)
                dve.sem_inc(sw_ready, 1)
                dve.sem_inc(added, 1)

                def add(n, first):
                    dve.wait_ge(combined, first + (n + 2))
                    dve.tensor_tensor(acc[:, n], acc[:, n], psum[:, 4 + n % 2, 0:T], ALU.add).then_inc(added, 1)

                with dve.Fori(0, R * (PAIRS // 2)) as q:
                    for u in range(2):
                        it = q * 2 + u
                        dve.wait_ge(idx_ready, it + 1)
                        dve.tensor_scalar(sw[:, u], token_no, meta[:, u, 1:2], meta[:, u, 0:1], ALU.is_equal, ALU.mult).then_inc(sw_ready, 1)
                        dve.wait_ge(selected, it + 1)
                        dve.wait_ge(shifted, it + 2)
                        select(u, (it + 2) % PAIRS, it + 3)
                        dve.wait_ge(added, it * KC + 1)
                        for n in range(2):
                            add(n, it * KC)
                        dve.wait_ge(silu_done, it + 1)
                        dve.tensor_tensor(h_sl, sil_sl, psum[:, u, F:2 * F], ALU.mult).then_inc(hx_ready, 1)
                        for n in range(2, KC):
                            add(n, it * KC)
                        dve.wait_ge(selected, it + 3)
                        dve.wait_ge(turned, it + 1)
                        dve.wait_ge(sw_ready, it + 2)
                        indices(u, it * 3 + 6)
                last = dve.snap(R * (PAIRS * KC))
                dve.wait_ge(added, last + 1)
                for n in range(KC):
                    add(n, last)
                dve.wait_ge(added, last + (KC + 1))
                norm(1, acc)
                for n in range(KC):
                    dve.tensor_scalar(x1[:, n], acc[:, n], vec[:, V_LN + 2 * KC + n:V_LN + 2 * KC + n + 1],
                                      vec[:, V_LN + 3 * KC + n:V_LN + 3 * KC + n + 1], ALU.mult, ALU.add).then_inc(y_ready, 1)

            @block.tensor
            def _(pe):
                def strip(slot, loads, n2, par, rhs):
                    pe.wait_ge(slot_loaded[slot], loads)
                    pe.wait_ge(bank_free[par], n2)
                    for k in range(KC):
                        ins = pe.matmul(psum[:, 5 + par, 0:T], ring[:, slot, k], rhs[:, k], start=(k == 0), stop=(k == KC - 1))
                    ins.then_inc(strips_done, 1)

                for layer, (rhs, ready) in enumerate(((xcb, v_ready), (ys, z_ready), (us, glu_ready), (ys, m_ready))):
                    pe.wait_ge(ready, 1)
                    with pe.Fori(0, 2) as g:
                        for j in range(4):
                            strip(j, g * 16 + (16 * (2 + NSEG + 2 * layer + 1)), g * 2 + (3 * KC + 4 * layer + j // 2), j % 2, rhs)

                def column_sums(src):
                    for k in range(KC):
                        ins = pe.matmul(psum[:, 4, 0:T], ones[:], src[:, k], start=(k == 0), stop=(k == KC - 1))
                    ins.then_inc(stat_out, 1)

                for b in range(2):
                    pe.wait_ge(bank_free[b], 3 * KC + 16)
                column_sums(r_)
                pe.wait_ge(stat_in, 1)
                column_sums(sq)
                pe.wait_ge(x1_ready, 1)
                pe.wait_ge(router_loaded, 16)
                for c in range(TC):
                    for k in range(KC):
                        ins = pe.matmul(psum[0:tok[c], 7, c * E:c * E + E], x1[:, k, c * P:c * P + tok[c]], wr[:, k], start=(k == 0), stop=(k == KC - 1))
                    ins.then_inc(logits_ready, 1)
                for c in range(TC):
                    if c == 2:
                        pe.wait_ge(xrow_ready, 1)
                    for k in range(KC):
                        ins = pe.transpose(psum[0:tok[c], 2 * (c % 2) + k // 4, (k % 4) * P:(k % 4) * P + P], x1[:, k, c * P:c * P + tok[c]], ident[:])
                    ins.then_inc(xrow_turned, 1)
                pe.wait_ge(xrow_ready, TC)
                pe.wait_ge(gu_in[3], 16)
                for f in range(2 * FC):
                    for k in range(KC):
                        ins = pe.matmul(psum[:, f, 0:T], gu[:, 3, k, f * P:f * P + P], x1[:, k], start=(k == 0), stop=(k == KC - 1))
                    ins.then_inc(shared_gu, 1)
                pe.wait_ge(picks_ready, 1)
                for c in range(TC + 1):
                    for b in range(min(c + 1, TC)):
                        ins = pe.matmul(psum[:, 6, c * E:c * E + E], tri[:] if b == c else ones[:], pk[:, b], start=(b == 0), stop=(b == min(c, TC - 1)))
                ins.then_inc(counted, 1)

                def select(u, pair):
                    for c in range(TC):
                        ins = pe.matmul(psum[:, 6, 0:4], S[:, u, c], val[:, c, bass.ds(pair * 2, 2)].rearrange("p e v -> p (e v)"), start=(c == 0), stop=(c == TC - 1))
                    ins.then_inc(selected, 1)

                def turn(u):
                    for k in range(KC):
                        ins = pe.transpose(psum[:, 2 + k // 4, (k % 4) * P:(k % 4) * P + P], x_rows[:, u, k * P:k * P + P], ident[:])
                    ins.then_inc(turned, 1)

                R = n_rounds(pe)
                for u in range(2):
                    pe.wait_ge(select_ready, u + 1)
                    if u:
                        pe.wait_ge(idx_ready, u)
                    select(u, u)
                pe.wait_ge(shared_h, FC)
                pe.wait_ge(dn_in[3], 16)
                for n in range(KC):
                    if n > 1:
                        pe.wait_ge(shared_used, n - 1)
                    for f in range(FC):
                        ins = pe.matmul(psum[:, 4 + n % 2, 0:T], dn[:, 3, f, n * P:n * P + P], hT[:, f], start=(f == 0), stop=(f == FC - 1))
                    ins.then_inc(shared_dn, 1)
                pe.wait_ge(gathered[0], 16)
                turn(0)
                pe.wait_ge(shared_used, KC)
                pe.sem_inc(combined, 1)

                def combine(u, first):
                    for n in range(KC):
                        if n > 1:
                            pe.wait_ge(added, first + n)
                        pe.matmul(psum[:, 4 + n % 2, 0:T], y_rows[:, u, n * P:n * P + P], sw[:, u], start=True, stop=True).then_inc(combined, 1)

                with pe.Fori(0, R * (PAIRS // 2)) as q:
                    for u in range(2):
                        it = q * 2 + u
                        pe.wait_ge(xg_ready, it + 1)
                        for j in range(2):
                            s = 2 * u + j
                            pe.wait_ge(gu_in[s], q * 16 + (32 if s == 3 else 16))
                        for k in range(KC):
                            for j in range(2):
                                ins = pe.matmul(psum[SL * j:SL * j + SL, u, :], xg[:, u, k, SL * j:SL * j + SL], gu[:, 2 * u + j, k],
                                                start=(k == 0), stop=(k == KC - 1))
                        ins.then_inc(gu_done, 1)
                        pe.wait_ge(y_copied, it + 1)
                        pe.wait_ge(sw_ready, it + 1)
                        combine(1 - u, it * KC)
                        pe.wait_ge(gathered[1 - u], q * 16 + 16 * (u + 1))
                        turn(1 - u)
                        pe.wait_ge(select_ready, it + 3)
                        pe.wait_ge(idx_ready, it + 2)
                        select(u, (it + 2) % PAIRS)
                        pe.wait_ge(hx_ready, it + 2)
                        for f in range(FC):
                            ins = pe.transpose(psum[:, 7, f * P:f * P + P], h_sl[:, f * P:f * P + P], ident[:])
                        ins.then_inc(h_turned, 1)
                        for j in range(2):
                            s = 2 * u + j
                            pe.wait_ge(dn_in[s], q * 16 + (32 if s == 3 else 16))
                        pe.wait_ge(hT_ready, it + 1)
                        pe.wait_ge(added, it * KC + (KC + 1))
                        for h in range(2):
                            for f in range(FC):
                                for j in range(2):
                                    ins = pe.matmul(psum[SL * j:SL * j + SL, 4 + h, :], hT_sl[:, f, SL * j:SL * j + SL],
                                                    dn[:, 2 * u + j, f, h * 512:h * 512 + 512], start=(f == 0), stop=(f == FC - 1))
                        ins.then_inc(dn_done, 1)
                pairs = pe.snap(R * PAIRS)
                last = pe.snap(R * (PAIRS * KC))
                pe.wait_ge(y_copied, pairs + 1)
                pe.wait_ge(sw_ready, pairs + 1)
                combine(1, last)
                pe.wait_ge(added, last + (KC + 1))
                column_sums(acc)
                pe.wait_ge(stat_in, 2)
                column_sums(sq)


def kernel(x_prompt, x_sample, state_conv, state_ssm_re, state_ssm_im,
           w_in, b_in, conv_w, w_conv_out, a_re, a_im, log_dt,
           ssm_b_re, ssm_b_im, ssm_c_re, ssm_c_im, ssm_d, w_glu, b_glu, w_ssm_out, w_o,
           ln1_g, ln1_b, w_router, router_bias, w_gate, w_up, w_down,
           ws_gate, ws_up, ws_down, ln2_g, ln2_b):
    import concourse.bacc as bacc
    from concourse.bass_utils import run_bass_kernel_spmd

    def a(x):
        return np.asarray(x)

    def chunks(v):
        return np.moveaxis(a(v).reshape(v.shape[:-1] + (KC, P)), -1, 0)

    def strips(w):
        return a(w).reshape(KC, P, -1, P).transpose(2, 1, 0, 3)

    def by_state(v):
        v = a(v).reshape(v.shape[:-2] + (NT, P))
        return np.moveaxis(v, -1, 0)

    f32 = np.float32
    x = np.concatenate([a(x_prompt)[0], a(x_sample)[:, 0]], axis=0)
    secs = strips(w_in[0]).reshape(6, KC, P, KC, P)
    order = [3, 1, 2, 0, 4, 5]
    w_front = np.concatenate([secs[i] for i in order] + [strips(w[0]) for w in (w_conv_out, w_glu, w_ssm_out, w_o)], axis=0)
    bin_ = chunks(a(b_in)[0].reshape(6, D)[order])
    dt = np.repeat(a(log_dt)[0][:, None], N, axis=1)
    rb = np.repeat(a(router_bias)[0][None, :], P, axis=0)
    vecs = np.concatenate([bin_.reshape(P, -1), chunks(b_glu[0]), chunks(conv_w[0]).reshape(P, -1), chunks(ssm_d[0]),
                           chunks(ln1_g[0]), chunks(ln1_b[0]), chunks(ln2_g[0]), chunks(ln2_b[0]),
                           by_state(a_re[0]), by_state(a_im[0]), by_state(dt), rb], axis=1)
    b_sm = np.zeros((P, 2, NT, 32), f32)
    c_sm = np.zeros((P, 2, NT, 32), f32)
    for r, (b, c) in enumerate(((ssm_b_re, ssm_c_re), (ssm_b_im, ssm_c_im))):
        b = a(b)[0].reshape(NT, 2, N, H)
        c = a(c)[0].reshape(NT, 2, H, N)
        for g in range(2):
            b_sm[g * N:g * N + N, r, :, g * H:g * H + H] = b[:, g].transpose(1, 0, 2)
            c_sm[g * N:g * N + N, r, :, g * H:g * H + H] = c[:, g].transpose(2, 0, 1)
    h0 = np.stack([by_state(state_ssm_re[0]), by_state(state_ssm_im[0])], axis=1).transpose(0, 1, 3, 2)
    cs = chunks(state_conv[0]).transpose(0, 3, 2, 1)

    def experts_in(g, u, n):
        w = np.concatenate([a(g).reshape(n, KC, P, F), a(u).reshape(n, KC, P, F)], axis=3)
        return w.transpose(0, 2, 1, 3).reshape(n, P, KC * 2 * F)

    def experts_out(w, n):
        return a(w).reshape(n, FC, P, D).transpose(0, 2, 1, 3).reshape(n, P, FC * D)

    arrays = {
        "x_t": x.T.reshape(KC, P, T).transpose(1, 0, 2),
        "w_front": w_front.reshape(-1, P, KC * P),
        "vecs": vecs,
        "b_sm": b_sm,
        "c_sm": c_sm,
        "h0": h0,
        "conv_state": cs,
        "w_router": a(w_router)[0].reshape(KC, P, E).transpose(1, 0, 2),
        "w_gu": np.concatenate([experts_in(w_gate[0], w_up[0], E), experts_in(ws_gate[0], ws_up[0], 1)], axis=0),
        "w_dn": np.concatenate([experts_out(w_down[0], E), experts_out(ws_down[0], 1)], axis=0),
    }
    outs = {"o_y": (P, KC, T), "o_conv_p": (P, KC, 2), "o_conv_s": (P, KC, 2, NS), "o_ssm_p": (P, 2, NT), "o_ssm_s": (P, 2, NT, NS)}
    nc = bacc.Bacc("TRN2", target_bir_lowering=False, num_devices=1)
    args = {}
    for name in arrays:
        arrays[name] = np.ascontiguousarray(arrays[name])
        args[name] = nc.dram_tensor(name, arrays[name].shape, F32, kind="ExternalInput").ap()
    for name, shape in outs.items():
        args[name] = nc.dram_tensor(name, shape, F32, kind="ExternalOutput").ap()
    build(nc, **args)
    res = run_bass_kernel_spmd(nc, [arrays], core_ids=[0]).results[0]

    y = res["o_y"].transpose(2, 1, 0).reshape(T, D)
    conv_p = res["o_conv_p"].transpose(2, 1, 0).reshape(1, 1, 2, D)
    conv_s = res["o_conv_s"].transpose(3, 2, 1, 0).reshape(1, NS, 2, D)
    ssm_p = res["o_ssm_p"].transpose(1, 2, 0).reshape(2, 1, 1, G, N)
    ssm_s = res["o_ssm_s"].transpose(1, 3, 2, 0).reshape(2, 1, NS, G, N)
    c = np.ascontiguousarray
    return (c(y[:LP].reshape(1, LP, D)), c(y[LP:].reshape(NS, 1, D)), c(conv_p), c(ssm_p[0]), c(ssm_p[1]),
            c(conv_s), c(ssm_s[0]), c(ssm_s[1]))
```
